# Optimizing a Trainium2 kernel written in Bass

```python
import math
import jax, jax.numpy as jnp
from jax import lax
import numpy as np

D_MODEL = 1024
BATCH = 1
SEQ = 512
DEPTH = 1
DEC_BATCH = 1
DEC_SEQ = 1024
PAST_LEN = 128

N_HEADS_ATTN = 8
QK_NOPE_DIM = 64
QK_ROPE_DIM = 32
V_HEAD_DIM = 64
Q_LORA_RANK = 256
KV_LORA_RANK = 128
ROPE_THETA = 10000.0
Q_BLOCK = 128
D_ATTN = N_HEADS_ATTN * V_HEAD_DIM
N_HEADS_SSD = 8
SSD_HEAD_DIM = 64
D_SSD = N_HEADS_SSD * SSD_HEAD_DIM
SSD_GROUPS = 2
D_STATE = 64
D_CONV = 5
CHUNK = 128
CONV_DIM = D_SSD + 2 * SSD_GROUPS * D_STATE
D_MIX = D_ATTN + D_SSD
D_IN_PROJ = Q_LORA_RANK + KV_LORA_RANK + QK_ROPE_DIM + D_SSD + CONV_DIM + 2 * N_HEADS_SSD
N_EXPERTS = 16
CAPACITY_FACTOR = 2
D_EXPERT = 2048
N_MOD = 6
EPS = 1e-6

kernel_name = 'hymba_mla_ssd_ec_moe_encoder'

def _rms(x):
    xf = x.astype(jnp.float32)
    return xf * lax.rsqrt(jnp.mean(xf * xf, axis=-1, keepdims=True) + EPS)

def _rmsnorm(x, w):
    return (_rms(x) * w.astype(jnp.float32)).astype(x.dtype)

def _rope_tables(seq, dtype):
    pos = jnp.arange(seq, dtype=jnp.float32)
    inv = 1.0 / (ROPE_THETA ** (jnp.arange(0, QK_ROPE_DIM, 2, dtype=jnp.float32) / QK_ROPE_DIM))
    ang = pos[:, None] * inv[None, :]
    return jnp.cos(ang).astype(dtype), jnp.sin(ang).astype(dtype)

def _rope(x, cos, sin):
    x1, x2 = jnp.split(x, 2, axis=-1)
    return jnp.concatenate([x1 * cos - x2 * sin, x2 * cos + x1 * sin], axis=-1)

def _mla(cq, ckv, kr, q_norm_w, w_uq, kv_norm_w, w_ukv, attn_norm_w):
    b, s, _ = cq.shape
    cos, sin = _rope_tables(s, cq.dtype)
    q = (_rmsnorm(cq, q_norm_w) @ w_uq).reshape(b, s, N_HEADS_ATTN, QK_NOPE_DIM + QK_ROPE_DIM)
    q_nope, q_rope = jnp.split(q, [QK_NOPE_DIM], axis=-1)
    q_rope = _rope(q_rope, cos[:, None, :], sin[:, None, :])
    kv = (_rmsnorm(ckv, kv_norm_w) @ w_ukv).reshape(b, s, N_HEADS_ATTN, QK_NOPE_DIM + V_HEAD_DIM)
    k_nope, v = jnp.split(kv, [QK_NOPE_DIM], axis=-1)
    k_rope = _rope(kr, cos, sin)
    scale = (QK_NOPE_DIM + QK_ROPE_DIM) ** -0.5
    nb = s // Q_BLOCK

    def to_blocks(t):
        return jnp.moveaxis(t.reshape(b, nb, Q_BLOCK, N_HEADS_ATTN, t.shape[-1]), 1, 0)

    def attend(blk):
        qn, qr = blk
        sc = jnp.einsum('bqhd,bkhd->bhqk', qn, k_nope) + jnp.einsum('bqhr,bkr->bhqk', qr, k_rope)
        p = jax.nn.softmax(sc.astype(jnp.float32) * scale, axis=-1).astype(v.dtype)
        return jnp.einsum('bhqk,bkhd->bqhd', p, v)

    o = lax.map(attend, (to_blocks(q_nope), to_blocks(q_rope)))
    o = jnp.moveaxis(o, 0, 1).reshape(b, s, D_ATTN)
    return _rmsnorm(o, attn_norm_w)

def _dwconv(u, w, bias):
    out = lax.conv_general_dilated(u, w[:, None, :], window_strides=(1,),
                                   padding=[(D_CONV // 2, D_CONV // 2)],
                                   dimension_numbers=('NWC', 'WIO', 'NWC'),
                                   feature_group_count=u.shape[-1])
    return out + bias

def _ssd_scan(x, dt, a, bm, cm):
    b, l, nh, p = x.shape
    g, n = bm.shape[2], bm.shape[3]
    r = nh // g
    nc = l // CHUNK
    x = x.astype(jnp.float32).reshape(b, nc, CHUNK, g, r, p)
    dt = dt.reshape(b, nc, CHUNK, g, r)
    bm = bm.astype(jnp.float32).reshape(b, nc, CHUNK, g, n)
    cm = cm.astype(jnp.float32).reshape(b, nc, CHUNK, g, n)
    cs = jnp.cumsum(dt * a.reshape(g, r), axis=2)
    lower = jnp.tril(jnp.ones((CHUNK, CHUNK), bool))[None, None, :, :, None, None]
    seg = cs[:, :, :, None] - cs[:, :, None, :]
    decay_in = jnp.exp(jnp.where(lower, seg, -jnp.inf))
    cb = jnp.einsum('bcqgn,bcsgn->bcqsg', cm, bm)
    m = cb[..., None] * decay_in * dt[:, :, None]
    y_diag = jnp.einsum('bcqsgr,bcsgrp->bcqgrp', m, x)
    decay_out = jnp.exp(cs[:, :, -1:] - cs)
    states = jnp.einsum('bcsgn,bcsgr,bcsgrp->bcgrpn', bm, decay_out * dt, x)
    chunk_decay = jnp.exp(cs[:, :, -1])

    def step(carry, inp):
        st, dec = inp
        return carry * dec[..., None, None] + st, carry

    init = jnp.zeros((b, g, r, p, n), jnp.float32)
    _, s_in = lax.scan(step, init, (jnp.moveaxis(states, 1, 0), jnp.moveaxis(chunk_decay, 1, 0)))
    s_in = jnp.moveaxis(s_in, 0, 1)
    y_off = jnp.einsum('bcqgn,bcgrpn->bcqgrp', cm, s_in) * jnp.exp(cs)[..., None]
    return (y_diag + y_off).reshape(b, l, nh, p)

def _ssd_mixer(z, xbc, dt_raw, conv_w, conv_b, a_log, dt_bias, d_skip, ssd_norm_w):
    b, s, _ = z.shape
    f32 = jnp.float32
    xbc = jax.nn.silu(_dwconv(xbc, conv_w, conv_b))
    xs, bm, cm = jnp.split(xbc, [D_SSD, D_SSD + SSD_GROUPS * D_STATE], axis=-1)
    xh = xs.reshape(b, s, N_HEADS_SSD, SSD_HEAD_DIM)
    bm = bm.reshape(b, s, SSD_GROUPS, D_STATE)
    cm = cm.reshape(b, s, SSD_GROUPS, D_STATE)
    dt = jax.nn.softplus(dt_raw.astype(f32).reshape(b, s, 2, N_HEADS_SSD) + dt_bias.astype(f32))
    a = -jnp.exp(a_log.astype(f32))
    flip = lambda t: jnp.flip(t, axis=1)
    y_fwd = _ssd_scan(xh, dt[:, :, 0], a[0], bm, cm)
    y_bwd = flip(_ssd_scan(flip(xh), flip(dt[:, :, 1]), a[1], flip(bm), flip(cm)))
    y = y_fwd + y_bwd + d_skip.astype(f32)[:, None] * xh.astype(f32)
    y = y.reshape(b, s, D_SSD) * jax.nn.silu(z.astype(f32))
    y = _rms(y.reshape(b, s, SSD_GROUPS, D_SSD // SSD_GROUPS)).reshape(b, s, D_SSD)
    return (y * ssd_norm_w.astype(f32)).astype(z.dtype)

def _ec_moe(h, w_router, w_gate, w_up, w_down):
    b, s, d = h.shape
    t = b * s
    tok = h.reshape(t, d)
    aff = jax.nn.softmax((tok @ w_router).astype(jnp.float32), axis=-1)
    cap = max(1, CAPACITY_FACTOR * t // N_EXPERTS)
    gate, idx = lax.top_k(aff.T, cap)
    xe = tok[idx]
    hid = jax.nn.silu(jnp.einsum('ecd,edf->ecf', xe, w_gate)) * jnp.einsum('ecd,edf->ecf', xe, w_up)
    ye = jnp.einsum('ecf,efd->ecd', hid, w_down) * gate[..., None].astype(h.dtype)
    out = jnp.zeros_like(tok).at[idx.reshape(-1)].add(ye.reshape(-1, d))
    return out.reshape(b, s, d)

def _layer(x, c, w_ada, b_ada, norm1_w, w_in, q_norm_w, w_uq, kv_norm_w, w_ukv, attn_norm_w,
           conv_w, conv_b, a_log, dt_bias, d_skip, ssd_norm_w, w_out, norm2_w,
           w_router, w_gate, w_up, w_down):
    mod = jax.nn.silu(c) @ w_ada + b_ada
    sh1, sc1, g1, sh2, sc2, g2 = jnp.split(mod[:, None, :], N_MOD, axis=-1)
    h = _rmsnorm(x, norm1_w) * (1.0 + sc1) + sh1
    proj = h @ w_in
    offs = np.cumsum([Q_LORA_RANK, KV_LORA_RANK, QK_ROPE_DIM, D_SSD, CONV_DIM]).tolist()
    cq, ckv, kr, z, xbc, dt_raw = jnp.split(proj, offs, axis=-1)
    y_attn = _mla(cq, ckv, kr, q_norm_w, w_uq, kv_norm_w, w_ukv, attn_norm_w)
    y_ssd = _ssd_mixer(z, xbc, dt_raw, conv_w, conv_b, a_log, dt_bias, d_skip, ssd_norm_w)
    x = x + g1 * (jnp.concatenate([y_attn, y_ssd], axis=-1) @ w_out)
    h = _rmsnorm(x, norm2_w) * (1.0 + sc2) + sh2
    return x + g2 * _ec_moe(h, w_router, w_gate, w_up, w_down)

def setup_inputs(seed: int = 0) -> dict:
    key = jax.random.key(seed)
    ks = jax.random.split(key, 32)
    f32 = jnp.float32
    nrm = lambda k, shape, sc: jax.random.normal(k, shape, f32) * sc
    gain = lambda k, shape: 1.0 + 0.05 * jax.random.normal(k, shape, f32)
    L = DEPTH
    dt0 = jnp.exp(jax.random.uniform(ks[14], (L, 2, N_HEADS_SSD), f32, math.log(1e-3), math.log(1e-1)))
    return {
        'x_prompt': nrm(ks[0], (BATCH, SEQ, D_MODEL), 1.0),
        'x_sample': nrm(ks[1], (DEC_BATCH, DEC_SEQ, D_MODEL), 1.0),
        'c_prompt': nrm(ks[2], (BATCH, D_MODEL), 1.0),
        'c_sample': nrm(ks[3], (DEC_BATCH, D_MODEL), 1.0),
        'w_ada': nrm(ks[4], (L, D_MODEL, N_MOD * D_MODEL), 0.5 * D_MODEL ** -0.5),
        'b_ada': nrm(ks[5], (L, N_MOD * D_MODEL), 0.01),
        'norm1_w': gain(ks[6], (L, D_MODEL)),
        'w_in': nrm(ks[7], (L, D_MODEL, D_IN_PROJ), D_MODEL ** -0.5),
        'q_norm_w': gain(ks[8], (L, Q_LORA_RANK)),
        'w_uq': nrm(ks[9], (L, Q_LORA_RANK, N_HEADS_ATTN * (QK_NOPE_DIM + QK_ROPE_DIM)), Q_LORA_RANK ** -0.5),
        'kv_norm_w': gain(ks[10], (L, KV_LORA_RANK)),
        'w_ukv': nrm(ks[11], (L, KV_LORA_RANK, N_HEADS_ATTN * (QK_NOPE_DIM + V_HEAD_DIM)), KV_LORA_RANK ** -0.5),
        'attn_norm_w': gain(ks[12], (L, D_ATTN)),
        'conv_w': nrm(ks[13], (L, D_CONV, CONV_DIM), D_CONV ** -0.5),
        'conv_b': nrm(ks[15], (L, CONV_DIM), 0.01),
        'a_log': jnp.log(jax.random.uniform(ks[16], (L, 2, N_HEADS_SSD), f32, 1.0, 16.0)),
        'dt_bias': dt0 + jnp.log(-jnp.expm1(-dt0)),
        'd_skip': gain(ks[17], (L, N_HEADS_SSD)),
        'ssd_norm_w': gain(ks[18], (L, D_SSD)),
        'w_out': nrm(ks[19], (L, D_MIX, D_MODEL), D_MIX ** -0.5),
        'norm2_w': gain(ks[20], (L, D_MODEL)),
        'w_router': nrm(ks[21], (L, D_MODEL, N_EXPERTS), D_MODEL ** -0.5),
        'w_gate': nrm(ks[22], (L, N_EXPERTS, D_MODEL, D_EXPERT), D_MODEL ** -0.5),
        'w_up': nrm(ks[23], (L, N_EXPERTS, D_MODEL, D_EXPERT), D_MODEL ** -0.5),
        'w_down': nrm(ks[24], (L, N_EXPERTS, D_EXPERT, D_MODEL), D_EXPERT ** -0.5),
        'final_norm_w': gain(ks[25], (D_MODEL,)),
    }

def reference(x_prompt, x_sample, c_prompt, c_sample, w_ada, b_ada, norm1_w, w_in,
              q_norm_w, w_uq, kv_norm_w, w_ukv, attn_norm_w, conv_w, conv_b, a_log,
              dt_bias, d_skip, ssd_norm_w, w_out, norm2_w, w_router, w_gate, w_up,
              w_down, final_norm_w):
    layer_params = (w_ada, b_ada, norm1_w, w_in, q_norm_w, w_uq, kv_norm_w, w_ukv, attn_norm_w,
                    conv_w, conv_b, a_log, dt_bias, d_skip, ssd_norm_w, w_out, norm2_w,
                    w_router, w_gate, w_up, w_down)

    def trunk(x, c):
        for i in range(DEPTH):
            x = _layer(x, c, *[prm[i] for prm in layer_params])
        return _rmsnorm(x, final_norm_w)

    y_prompt = trunk(x_prompt, c_prompt)
    y_sample = trunk(x_sample, c_sample)
    return (y_prompt, y_sample)


_drawn_inputs = setup_inputs


def setup_inputs(seed=0):
    import zlib

    import numpy as np

    out = dict(_drawn_inputs(seed))
    spreads = {}
    factors = {'b_ada': 3.719,
     'norm1_w': 3.203,
     'q_norm_w': 8.0,
     'kv_norm_w': 4.241,
     'attn_norm_w': 5.35,
     'conv_b': 8.0,
     'd_skip': 148.817,
     'ssd_norm_w': 4.385,
     'norm2_w': 5.853}
    for name, (base, spread) in spreads.items():
        noise = np.random.default_rng([zlib.crc32(name.encode()), seed]).standard_normal(out[name].shape)
        drawn = base * np.exp(spread * noise) if base else spread * noise
        out[name] = __import__('jax').numpy.asarray(drawn.astype(out[name].dtype))
    for name, factor in factors.items():
        out[name] = (out[name] * factor).astype(out[name].dtype)
    return out
```

```python
from contextlib import ExitStack

import concourse.bass as bass
from concourse import mybir

ALU = mybir.AluOpType
ACT = mybir.ActivationFunctionType
AX_X = mybir.AxisListType.X
F32 = mybir.dt.float32
U32 = mybir.dt.uint32

P = 128
D = 1024
KD = D // P
T_OF = (512, 1024)
NT = sum(T_OF) // P
TILES = ((0, 4), (4, 12))
NH, DN, DR, DV = 8, 64, 32, 64
DQK = DN + DR
QL, KVL = 256, 128
NS, HP, DS = 8, 64, 64
DSSD = NS * HP
CONV = DSSD + 2 * 2 * DS
KC = CONV // P
TAPS = 5
NAT = QL + KVL + DR
Z0, X0, DT0 = NAT, NAT + DSSD, NAT + DSSD + CONV
DIN = DT0 + 2 * NS
NE, FE = 16, 2048
CAP = (64, 128)
EPS = 1e-6
SCALE = float(DQK) ** -0.5
SPANS = ((0, 2, 0), (2, 4, 0), (4, 10, 1), (10, 12, 1))

COLS = {}
_at = 0
for _name, _n in (("c", 2 * KD), ("norm1", KD), ("norm2", KD), ("final", KD), ("q_norm", 2), ("kv_norm", 1),
                  ("attn_norm", 4), ("ssd_norm", 4), ("conv_b", KC), ("conv_w", TAPS * KC), ("b_ada", 6 * KD)):
    COLS[_name] = (_at, _at + _n)
    _at += _n
NCOL = _at
ROW_DTB, ROW_ALOG, ROW_D, NROW = 0, 16, 32, 40
M_ID, M_LE, M_GT, M_GE, M_LT, M_ONE = range(6)
D_CSF, D_CSB, D_OUTF, D_OUTB, D_TOT = range(5)
PADT = 4
XW = NT * P + 2 * PADT


def tile_loop(eng, body):
    for lo, hi, request in SPANS:
        if hi - lo == 2:
            body(lo, 0, request)
            body(lo + 1, 1, request)
        else:
            with eng.Fori(lo // 2, hi // 2) as turn:
                body(turn * 2, 0, request)
                body(turn * 2 + 1, 1, request)


def tile_loop_ahead(eng, front, back):
    front(0, 0, 0)
    for lo, hi, request in SPANS:
        def pair(g, after):
            front(g + 1, 1, request)
            back(g, 0, request)
            if after is not None:
                front(g + 2, 0, after)
            back(g + 1, 1, request)
        if hi - lo == 2:
            pair(lo, None if hi == NT else 1 if hi == TILES[1][0] else request)
        else:
            with eng.Fori(lo // 2, hi // 2) as turn:
                pair(turn * 2, request)


def wait_apart(eng, sem, value, turns):
    eng.wait_ge(sem, value)
    eng.sem_inc(turns, 1)


class Order:

    def __init__(self, eng, sem, base=0):
        self.eng, self.sem, self.base, self.n = eng, sem, base, 0

    def link(self, ins):
        self.n += 1
        ins.then_inc(self.sem, 1)
        self.eng.wait_ge(self.sem, self.base + self.n)


class Core:

    def __init__(self, nc, ctx, io):
        self.nc, self.ctx, self.io = nc, ctx, io
        self.banks = ctx.enter_context(nc.psum_tensor("banks", [P, 8 * 512], F32))
        self.ps = [self.banks[:, 512 * i:512 * i + 512] for i in range(8)]
        self.masks = self.sbuf("masks", [P, 6, P])
        self.cols = self.sbuf("cols", [P, NCOL])
        self.rows = self.sbuf("rows", [P, NROW])
        self.rope = self.sbuf("rope", [P, 8, 2, 16])
        self.mod = self.sbuf("mod", [P, 6 * KD, 2])
        self.scale1 = self.sbuf("scale1", [P, KD, 2])
        self.scale2 = self.sbuf("scale2", [P, KD, 2])
        self.eps = self.sbuf("eps", [P, 2])
        self.tot = self.sbuf("chunk_decay", [P, NT, 2, 4])
        self.chosen = self.sbuf("chosen", [P, 48], U32)
        self.gates = self.sbuf("gates", [P, 48])
        self.residual, self.normed = self.dram("residual", [NT * P, D]), self.dram("normed", [NT * P, D])
        self.sems = {}
        self.ident = self.masks[:, M_ID, :]

    def sbuf(self, name, shape, dtype=F32):
        return self.ctx.enter_context(self.nc.sbuf_tensor(name, shape, dtype))

    def small(self, name, shape, dtype=F32):
        return self.stage.enter_context(self.nc.sbuf_tensor(name, shape, dtype))

    def sem(self, name):
        if name not in self.sems:
            self.sems[name] = self.nc.alloc_semaphore(name)
        return self.sems[name]

    def release(self):
        self.nc.clear_and_free_semaphores(list(self.sems.values()))
        self.nc.all_engine_barrier()
        self.sems = {}

    def col(self, name, k=0):
        a, _ = COLS[name]
        return self.cols[:, a + k:a + k + 1]

    def dram(self, name, shape):
        return self.nc.dram_tensor(name, shape, F32, kind="Internal").ap()


class Arena:

    def __init__(self, tensor, size):
        self.t, self.size = tensor, size

    def at(self, start, *dims):
        n = 1
        for d in dims:
            n *= d
        assert start + n <= self.size, (start, n, self.size)
        v = self.t[:, start:start + n]
        names = ["a", "b", "c", "d"][:len(dims)]
        if len(dims) == 1:
            return v
        return v.rearrange(f"p ({' '.join(names)}) -> p {' '.join(names)}", **dict(zip(names, dims)))


ARENA = 49920
A_WIN = 0
A_X, A_XN, A_HT, A_JUNK = 13696, 15744, 17792, 19840
A_RING = 25984
A_NAT = 25984
A_DT = A_NAT + NAT * NT
A_Z = A_DT + 2 * NS * NT
A_XBC = A_Z + DSSD * NT
SLABS = 4


def modulation(core, A):
    nc, io, sem = core.nc, core.io, core.sem
    ring = [A.at(A_RING + 4096 * s, KD, 512) for s in range(SLABS)]
    slab_in = [sem(f"ada_slab_in{s}") for s in range(SLABS)]
    slab_used, silu_c, mod_sum, consts_in = sem("ada_slab_used"), sem("silu_c"), sem("mod_sum"), sem("consts_in")
    dve_order = sem("mod_dve_order")
    sc = core.small("silu_c_cols", [P, KD, 2])
    w = io["w_ada"][0].rearrange("(k p) n -> p k n", p=P)
    c_cols = core.cols[:, 0:2 * KD].rearrange("p (r k) -> p k r", r=2)

    with nc.Block() as block:
        @block.sync
        def _(sp):
            for name, t in (("p_masks", core.masks), ("p_cols", core.cols), ("p_rows", core.rows), ("p_rope", core.rope)):
                sp.dma_start(t[:], io[name]).then_inc(consts_in, 16)
            for s in range(SLABS):
                sp.dma_start(ring[s], w[:, :, s * 512:s * 512 + 512]).then_inc(slab_in[s], 16)
            with sp.Fori(1, 12 // SLABS) as turn:
                for s in range(SLABS):
                    sp.wait_ge(slab_used, turn * SLABS + (s + 1 - SLABS))
                    sp.dma_start(ring[s], w[:, :, bass.ds((turn * SLABS + s) * 512, 512)]).then_inc(slab_in[s], 16)
            w_in = A.at(A_WIN, KD, DIN)
            src = io["w_in"][0].rearrange("(k p) n -> p k n", p=P)
            for h in range(2):
                sp.dma_start(w_in[:, 4 * h:4 * h + 4, :], src[:, 4 * h:4 * h + 4, :]).then_inc(sem("w_in_in"), 16)

        @block.scalar
        def _(act):
            act.wait_ge(consts_in, 64)
            nc.scalar.activation(sc[:], c_cols, ACT.Silu).then_inc(silu_c, 1)

        @block.tensor
        def _(pe):
            pe.wait_ge(silu_c, 1)
            with pe.Fori(0, 12 // SLABS) as turn:
                for s in range(SLABS):
                    pe.wait_ge(slab_in[s], turn * 16 + 16)
                    pe.wait_ge(mod_sum, turn * SLABS + (s + 1))
                    for c in range(4):
                        for k in range(KD):
                            mm = nc.tensor.matmul(core.ps[s][:, 2 * c:2 * c + 2],
                                                  ring[s][:, k, c * P:(c + 1) * P], sc[:, k, :],
                                                  start=(k == 0), stop=(k == KD - 1))
                    mm.then_inc(slab_used, 1)

        @block.vector
        def _(dve):
            order = Order(dve, dve_order)
            dve.sem_inc(mod_sum, SLABS)
            nc.vector.memset(core.eps[:, 0:1], EPS)
            nc.vector.memset(core.eps[:, 1:2], 1.0)
            dve.wait_ge(consts_in, 64)
            b0, b1 = COLS["b_ada"]
            with dve.Fori(0, 12 // SLABS) as turn:
                for s in range(SLABS):
                    dve.wait_ge(slab_used, turn * SLABS + (s + 1))
                    bias = core.cols[:, bass.ds(turn * (4 * SLABS) + (b0 + 4 * s), 4)]
                    nc.vector.tensor_tensor(core.mod[:, bass.ds(turn * (4 * SLABS) + 4 * s, 4), :],
                                            core.ps[s][:, 0:8].rearrange("p (j r) -> p j r", r=2),
                                            bias.unsqueeze(2).broadcast_to([P, 4, 2]), ALU.add).then_inc(mod_sum, 1)
            dve.wait_ge(mod_sum, SLABS + 12)
            for name, out, at in (("norm1", core.scale1, KD), ("norm2", core.scale2, 4 * KD)):
                n0, n1 = COLS[name]
                gain = core.cols[:, n0:n1].unsqueeze(2).broadcast_to([P, KD, 2])
                order.link(nc.vector.tensor_scalar(out[:], core.mod[:, at:at + KD, :], 1.0, None, ALU.add))
                order.link(nc.vector.tensor_tensor(out[:], out[:], gain, ALU.mult))


def load_tile(sp, dst, x_of, g, request, sem):
    return sp.dma_start(dst, x_of[request][0][bass.ds((g - TILES[request][0]) * P, P), :]).then_inc(sem, 16)


def projections(core, A):
    nc, io, sem = core.nc, core.io, core.sem
    w_in = A.at(A_WIN, KD, DIN)
    x = [A.at(A_X + D * j, D) for j in range(2)]
    xn = [A.at(A_XN + D * j, D) for j in range(2)]
    hT = [A.at(A_HT + D * j, KD, P) for j in range(2)]
    junk = A.at(A_JUNK, D)
    nat = A.at(A_NAT, NT * NAT)
    dt = A.at(A_DT, NT * 2 * NS)
    z = A.at(A_Z, NT * DSSD)
    xbc = A.at(A_XBC, KC, XW)
    ss, rms, rstd = (core.small(f"proj_{n}", [P, 2]) for n in ("ss", "rms", "rstd"))
    x_in = [sem(f"x_in{j}") for j in range(2)]
    sumsq, root, x_free, xn_ready = sem("x_sumsq"), sem("x_root"), sem("x_free"), sem("xn_ready")
    turned, hT_act, hT_dve = sem("xn_turned"), sem("hT_act"), sem("hT_dve")
    nat_done, z_done, xbc_done = sem("nat_done"), sem("z_done"), sem("xbc_done")
    banks_act, banks_dve = sem("proj_banks_act"), sem("proj_banks_dve")
    dve_order = sem("proj_dve_order")
    x_of = (io["x_prompt"], io["x_sample"])
    b_nat, b_z, b_x = core.ps[2], core.ps[3], core.ps[4:6]

    with nc.Block() as block:
        @block.sync
        def _(sp):
            def body(g, j, r):
                sp.wait_ge(x_free, g + 1)
                load_tile(sp, x[j], x_of, g, r, x_in[j])
            tile_loop(sp, body)

        @block.scalar
        def _(act):
            act.sem_inc(banks_act, 1)

            def stats(g, j):
                act.wait_ge(x_in[j], (g - j) * 8 + 16)
                nc.scalar.activation(junk, x[j], ACT.Square, accum_out=ss[:, j:j + 1]).then_inc(sumsq, 1)
                act.wait_ge(sumsq, g + 1)
                nc.scalar.activation(rms[:, j:j + 1], ss[:, j:j + 1], ACT.Sqrt, bias=core.eps[:, 0:1],
                                     scale=1.0 / D).then_inc(root, 1)

            def shift(g, j, r):
                act.wait_ge(turned, g + 1)
                for k in range(4):
                    ins = nc.scalar.activation(hT[j][:, k, :], core.ps[0][:, k * P:(k + 1) * P], ACT.Identity,
                                               bias=core.mod[:, k, r:r + 1], scale=core.scale1[:, k, r:r + 1])
                ins.then_inc(hT_act, 1)

            def body(g, j, r):
                stats(g, j)
                shift(g, j, r)
                act.wait_ge(nat_done, g + 1)
                nc.scalar.activation(nat[:, bass.ds(g * NAT, NAT)], b_nat[:, 0:NAT], ACT.Copy)
                nc.scalar.activation(dt[:, bass.ds(g * 16, 16)], b_nat[:, NAT:NAT + 16], ACT.Copy)
                act.wait_ge(z_done, g + 1)
                nc.scalar.activation(z[:, bass.ds(g * DSSD, DSSD)], b_z[:, :], ACT.Copy).then_inc(banks_act, 1)
            tile_loop(act, body)

        @block.vector
        def _(dve):
            dve.sem_inc(x_free, 2)
            dve.sem_inc(banks_dve, 1)
            for at in (0, 4 * P + 2, 4 * P + 4, XW - 2):
                nc.vector.memset(xbc[:, :, at:at + 2], 0.0)

            def body(g, j, r):
                dve.wait_ge(root, g + 1)
                nc.vector.reciprocal(rstd[:, j:j + 1], rms[:, j:j + 1]).then_inc(dve_order, 1)
                dve.wait_ge(dve_order, g + 1)
                nc.vector.tensor_scalar(xn[j], x[j], rstd[:, j:j + 1], None, ALU.mult).then_inc(xn_ready, 1)
                dve.wait_ge(xn_ready, g + 1)
                dve.sem_inc(x_free, 1)
                dve.wait_ge(turned, g + 1)
                for k in range(4, KD):
                    ins = nc.vector.tensor_scalar(hT[j][:, k, :], core.ps[1][:, (k - 4) * P:(k - 3) * P],
                                                  core.scale1[:, k, r:r + 1], core.mod[:, k, r:r + 1],
                                                  ALU.mult, ALU.add)
                ins.then_inc(hT_dve, 1)
                dve.wait_ge(xbc_done, g + 1)
                for c in range(2):
                    ins = nc.vector.tensor_copy(xbc[:, 3 * c:3 * c + 3, bass.ds(g * P + (2 + 4 * r), P)],
                                                b_x[c][:, 0:3 * P].rearrange("p (c t) -> p c t", c=3))
                ins.then_inc(banks_dve, 1)
            tile_loop(dve, body)

        @block.tensor
        def _(pe):
            pe.wait_ge(sem("w_in_in"), 32)

            def body(g, j, r):
                pe.wait_ge(xn_ready, g + 1)
                for k in range(KD):
                    mm = nc.tensor.transpose(core.ps[k // 4][:, k % 4 * P:(k % 4 + 1) * P],
                                             xn[j][:, k * P:(k + 1) * P], core.ident)
                mm.then_inc(turned, 1)
                pe.wait_ge(hT_act, g + 1)
                pe.wait_ge(hT_dve, g + 1)
                pe.wait_ge(banks_act, g + 1)
                for lo, hi, at in ((0, NAT, 0), (DT0, DIN, NAT)):
                    for k in range(KD):
                        mm = nc.tensor.matmul(b_nat[:, at:at + hi - lo], hT[j][:, k, :], w_in[:, k, lo:hi],
                                              start=(k == 0), stop=(k == KD - 1))
                mm.then_inc(nat_done, 1)
                for k in range(KD):
                    mm = nc.tensor.matmul(b_z[:, :], hT[j][:, k, :], w_in[:, k, Z0:X0],
                                          start=(k == 0), stop=(k == KD - 1))
                mm.then_inc(z_done, 1)
                pe.wait_ge(banks_dve, g + 1)
                for c in range(KC):
                    for k in range(KD):
                        mm = nc.tensor.matmul(b_x[c // 3][:, c % 3 * P:(c % 3 + 1) * P],
                                              w_in[:, k, X0 + c * P:X0 + (c + 1) * P], hT[j][:, k, :],
                                              start=(k == 0), stop=(k == KD - 1))
                mm.then_inc(xbc_done, 1)
            tile_loop(pe, body)


A_XC = 0
A_STB = 9216
A_STF = 13696
A_CT = A_STF + 256 * (NT + 2)
A_DEC = A_CT + NT * P
A_DTS = A_STB + 256 * (NT + 2)
A_DTA, A_W = A_DTS + 16 * NT, A_DTS + 32 * NT
A_XNAT = A_XBC
A_CB = A_XBC + DSSD * NT
A_TAIL = A_XBC + KC * XW
A_MIX = 13696
G16 = 16 * NT


def convolution(core, A):
    nc, sem = core.nc, core.sem
    xbc, xc = A.at(A_XBC, KC, XW), A.at(A_XC, KC, NT * P)
    z = A.at(A_Z, NT * DSSD)
    dt_raw, dt, dta, w = (A.at(a, NT, 16) for a in (A_DT, A_DTS, A_DTA, A_W))
    dec = A.at(A_DEC, 5, NT, 16)
    flat = [core.small(f"soft{i}", [P, NT, 16]) for i in range(4)]
    a_pos = core.small("a_pos", [P, 16])
    tot = core.tot
    tap0, tap_order = sem("conv_tap0"), sem("conv_order")
    soft_v, soft_e, soft_ln, steps, decays = (sem(n) for n in ("soft_v", "soft_e", "soft_ln", "steps", "decays"))
    dec_mm = sem("dec_mm")
    cw = COLS["conv_w"][0]
    seqs = [(2 + PADT * r + TILES[r][0] * P, T_OF[r], TILES[r][0] * P) for r in range(2)]

    with nc.Block() as block:
        @block.scalar
        def _(act):
            act.preload_act_table_set("natural_log_exp_and_others")
            act.wait_ge(soft_v, 1)
            nc.scalar.activation(flat[1][:], flat[1][:], ACT.Exp, scale=-1.0).then_inc(soft_e, 1)
            nc.scalar.activation(a_pos[:], core.rows[:, ROW_ALOG:ROW_ALOG + 16], ACT.Exp).then_inc(soft_e, 1)
            act.wait_ge(soft_v, 2)
            nc.scalar.activation(flat[3][:], flat[2][:], ACT.Ln).then_inc(soft_ln, 1)
            with act.Fori(0, KC) as c:
                for at, n, to in seqs:
                    nc.scalar.activation(xc[:, bass.ds(c, 1), to:to + n], xbc[:, bass.ds(c, 1), at - 2:at - 2 + n],
                                         ACT.Copy, scale=core.cols[:, bass.ds(c + cw, 1)]).then_inc(tap0, 1)
            act.wait_ge(dec_mm, 1)
            for kind in range(5):
                ins = nc.scalar.activation(dec[:, kind], core.ps[kind // 2][:, kind % 2 * G16:(kind % 2 + 1) * G16]
                                           .rearrange("p (g h) -> p g h", h=16), ACT.Exp)
            ins.then_inc(decays, 1)
            for q in range(4):
                n = NT * DSSD // 4
                nc.scalar.activation(z[:, q * n:(q + 1) * n], z[:, q * n:(q + 1) * n], ACT.Silu)

        @block.vector
        def _(dve):
            order = Order(dve, sem("soft_order"))
            v, m, one_e, ln = flat
            bias = core.rows[:, ROW_DTB:ROW_DTB + 16].unsqueeze(1).broadcast_to([P, NT, 16])
            order.link(nc.vector.tensor_tensor(v[:], dt_raw, bias, ALU.add))
            nc.vector.scalar_tensor_tensor(out=m[:], in0=v[:], scalar=-1.0, in1=v[:], op0=ALU.mult,
                                           op1=ALU.max).then_inc(soft_v, 1)
            dve.wait_ge(soft_e, 2)
            order.link(nc.vector.tensor_scalar(one_e[:], m[:], 1.0, None, ALU.add))
            dve.sem_inc(soft_v, 1)
            order.link(nc.vector.tensor_scalar(dta, one_e[:], -1.0, None, ALU.add))
            order.link(nc.vector.tensor_scalar(w, dta, 0.0, None, ALU.is_equal))
            order.link(nc.vector.tensor_tensor(dta, dta, w, ALU.add))
            order.link(nc.vector.reciprocal(dta, dta))
            order.link(nc.vector.tensor_tensor(dta, dta, m[:], ALU.mult))
            dve.wait_ge(soft_ln, 1)
            order.link(nc.vector.tensor_tensor(w, w, ln[:], ALU.add))
            order.link(nc.vector.tensor_tensor(w, w, dta, ALU.mult))
            order.link(nc.vector.scalar_tensor_tensor(out=dt, in0=v[:], scalar=0.0, in1=w, op0=ALU.max, op1=ALU.add))
            a = a_pos[:].unsqueeze(1).broadcast_to([P, NT, 16])
            nc.vector.scalar_tensor_tensor(out=dta, in0=dt, scalar=-1.0, in1=a, op0=ALU.mult,
                                           op1=ALU.mult).then_inc(steps, 1)
            with dve.Fori(0, KC) as c:
                for tap in range(1, TAPS):
                    for r, (at, n, to) in enumerate(seqs):
                        if tap == 1:
                            dve.wait_ge(tap0, c * 2 + (r + 1))
                        else:
                            dve.wait_ge(tap_order, c * 8 + (2 * (tap - 2) + r + 1))
                        out = xc[:, bass.ds(c, 1), to:to + n]
                        nc.vector.scalar_tensor_tensor(
                            out=out, in0=xbc[:, bass.ds(c, 1), at - 2 + tap:at - 2 + tap + n],
                            scalar=core.cols[:, bass.ds(c + (cw + tap * KC), 1)], in1=out,
                            op0=ALU.mult, op1=ALU.add).then_inc(tap_order, 1)
            dve.wait_ge(decays, 1)
            nc.vector.tensor_tensor(w[:, :, 0:8], dec[:, D_OUTF, :, 0:8], dt[:, :, 0:8], ALU.mult)
            nc.vector.tensor_tensor(w[:, :, 8:16], dec[:, D_OUTB, :, 8:16], dt[:, :, 8:16], ALU.mult)
            for half in range(2):
                rows = slice(64 * half, 64 * half + 64)
                src = dec[rows, D_TOT].rearrange("p g (d h) -> p g d h", d=2)[:, :, :, 4 * half:4 * half + 4]
                nc.vector.tensor_copy(tot[rows], src)

        @block.tensor
        def _(pe):
            pe.wait_ge(steps, 1)
            for kind, m in ((D_CSF, M_LE), (D_CSB, M_GE), (D_OUTF, M_GT), (D_OUTB, M_LT), (D_TOT, M_ONE)):
                mm = nc.tensor.matmul(core.ps[kind // 2][:, kind % 2 * G16:(kind % 2 + 1) * G16],
                                      core.masks[:, m, :], dta.rearrange("p g h -> p (g h)"), start=True, stop=True)
            mm.then_inc(dec_mm, 1)


def slot_in(g, r, back):
    return (g + (r + back)) * 256


def slot_out(g, r, back):
    return (g + (r + 1 - back)) * 256


def states(core, A):
    nc, sem = core.nc, core.sem
    xc = A.at(A_XC, KC, NT * P)
    ct = A.at(A_CT, NT * P)
    st = [A.at(A_STF, 256 * (NT + 2)), A.at(A_STB, 256 * (NT + 2))]
    w = A.at(A_W, G16)
    xnat, cb = A.at(A_XNAT, NT * DSSD), A.at(A_CB, NT * 256)
    xct = [A.at(A_TAIL + KC * P * j, KC, P) for j in range(2)]
    xw = A.at(A_TAIL + 2 * KC * P, 2, DSSD)
    bn = [core.small(f"b_nat{j}", [P, P]) for j in range(2)]
    btz = [core.small(f"b_groups{j}", [P, 2, P]) for j in range(2)]
    silu_done, btz_done, turned, cb_done = sem("silu_done"), sem("b_groups_done"), sem("x_turned"), sem("cb_done")
    xnat_done, xw_done, state_mm, state_out = sem("xnat_done"), sem("xw_done"), sem("state_mm"), sem("state_out")
    bn_done = sem("b_nat_done")

    with nc.Block() as block:
        @block.scalar
        def _(act):
            def front(g, j, r):
                for c in range(KC):
                    b = COLS["conv_b"][0] + c
                    ins = nc.scalar.activation(xct[j][:, c, :], xc[:, c, bass.ds(g * P, P)], ACT.Silu,
                                               bias=core.cols[:, b:b + 1])
                ins.then_inc(silu_done, 1)

            def back(g, j, r):
                act.wait_ge(turned, g + 1)
                nc.scalar.activation(xnat[:, bass.ds(g * DSSD, DSSD)], core.ps[j][:, :], ACT.Copy).then_inc(xnat_done, 1)
                act.wait_ge(cb_done, g + 1)
                act.wait_ge(bn_done, g + 1)
            tile_loop_ahead(act, front, back)

        @block.vector
        def _(dve):
            for t in btz:
                nc.vector.memset(t[0:64, 1, :], 0.0)
                nc.vector.memset(t[64:128, 0, :], 0.0)
            for r in range(2):
                lo, hi = TILES[r]
                nc.vector.memset(st[0][:, slot_in(lo, r, 0):slot_in(lo, r, 0) + 256], 0.0)
                nc.vector.memset(st[1][:, slot_in(hi - 1, r, 1):slot_in(hi - 1, r, 1) + 256], 0.0)

            def front(g, j, r):
                dve.wait_ge(silu_done, g + 1)
                nc.vector.tensor_copy(btz[j][0:64, 0, :], xct[j][0:64, 4, :])
                nc.vector.tensor_copy(btz[j][64:128, 1, :], xct[j][64:128, 4, :])
                nc.vector.tensor_copy(ct[:, bass.ds(g * P, P)], xct[j][:, 5, :]).then_inc(btz_done, 1)

            def back(g, j, r):
                dve.wait_ge(cb_done, g + 1)
                nc.vector.tensor_copy(cb[:, bass.ds(g * 256, 256)], core.ps[2 + j][:, P:3 * P])
                nc.vector.tensor_copy(bn[j][:], core.ps[2 + j][:, 0:P]).then_inc(bn_done, 1)
                dve.wait_ge(xnat_done, g + 1)
                for d in range(2):
                    nc.vector.tensor_tensor(
                        xw[:, d].rearrange("p (h e) -> p h e", h=NS),
                        xnat[:, bass.ds(g * DSSD, DSSD)].rearrange("p (h e) -> p h e", h=NS),
                        w[:, bass.ds(g * 16 + 8 * d, 8)].unsqueeze(2).broadcast_to([P, NS, HP]),
                        ALU.mult).then_inc(xw_done, 1)
                dve.wait_ge(state_mm, g + 1)
                for d in range(2):
                    ins = nc.vector.tensor_copy(st[d][:, bass.ds(slot_out(g, r, d), 256)], core.ps[4 + d][:, 0:256])
                ins.then_inc(state_out, 1)
            tile_loop_ahead(dve, front, back)

            dve.wait_ge(state_out, NT)
            scan(dve, nc, core, st, A.at(A_XC, 2, 256), sem("scan_order"), sem("scan_turns"))

        @block.tensor
        def _(pe):
            def front(g, j, r):
                pe.wait_ge(silu_done, g + 1)
                for c in range(4):
                    mm = nc.tensor.transpose(core.ps[j][:, c * P:(c + 1) * P], xct[j][:, c, :], core.ident)
                mm.then_inc(turned, 1)
                nc.tensor.transpose(core.ps[2 + j][:, 0:P], xct[j][:, 4, :], core.ident)
                pe.wait_ge(btz_done, g + 1)
                for grp in range(2):
                    mm = nc.tensor.matmul(core.ps[2 + j][:, (1 + grp) * P:(2 + grp) * P], btz[j][:, grp, :],
                                          xct[j][:, 5, :], start=True, stop=True)
                mm.then_inc(cb_done, 1)

            def back(g, j, r):
                pe.wait_ge(xw_done, g * 2 + 2)
                for d in range(2):
                    for grp in range(2):
                        mm = nc.tensor.matmul(core.ps[4 + d][64 * grp:64 * grp + 64, 0:256],
                                              bn[j][:, 64 * grp:64 * grp + 64], xw[:, d, 256 * grp:256 * grp + 256],
                                              start=True, stop=True)
                mm.then_inc(state_mm, 1)
            tile_loop_ahead(pe, front, back)


def scan(dve, nc, core, st, tmp, order, turns):
    dve.sem_inc(order, 2)
    tot = core.tot[:].rearrange("p g d h -> p (g d h)")
    done = 0
    for r, (lo, hi) in enumerate(TILES):
        with dve.Fori(0, hi - lo) as i:
            tiles = (i + lo, (hi - 1) - i)
            for d, g in enumerate(tiles):
                wait_apart(dve, order, i * 4 + (done + 1 + d), turns)
                decay = tot[:, bass.ds(g * 8 + 4 * d, 4)].unsqueeze(2).broadcast_to([P, 4, HP])
                nc.vector.tensor_tensor(tmp[:, d].rearrange("p (h e) -> p h e", h=4),
                                        st[d][:, bass.ds(slot_in(g, r, d), 256)].rearrange("p (h e) -> p h e", h=4),
                                        decay, ALU.mult).then_inc(order, 1)
            for d, g in enumerate(tiles):
                wait_apart(dve, order, i * 4 + (done + 3 + d), turns)
                out = st[d][:, bass.ds(slot_out(g, r, d), 256)]
                nc.vector.tensor_tensor(out, out, tmp[:, d], ALU.add).then_inc(order, 1)
        done += 4 * (hi - lo)


A_R, A_E, A_XDT, A_Y, A_CBM = 0, 2048, 4096, 5120, 8192


def ssd(core, A):
    nc, sem = core.nc, core.sem
    ct = A.at(A_CT, NT * P)
    st = [A.at(A_STF, 256 * (NT + 2)), A.at(A_STB, 256 * (NT + 2))]
    dt, dta = A.at(A_DTS, G16), A.at(A_DTA, G16)
    dec = A.at(A_DEC, 5, G16)
    z = A.at(A_Z, NT * DSSD)
    xnat, cb = A.at(A_XNAT, NT * DSSD), A.at(A_CB, NT * 256)
    mixT = A.at(A_MIX, 8, NT * P)
    r_sum = A.at(A_R, 2, NS, P)
    e = A.at(A_E, 2, NS, P)
    xdt = A.at(A_XDT, 2, NS, HP)
    y = A.at(A_Y, 5, DSSD)
    cbm = A.at(A_CBM, 2, 2, P)
    junk = A.at(A_TAIL, DSSD)
    ctz = [core.small(f"c_groups{j}", [P, 2, P]) for j in range(2)]
    ss, ln, rstd = (core.small(f"ssd_{n}", [P, 2]) for n in ("ss", "ln", "rstd"))
    r_done = [sem("seg_terms_f"), sem("seg_terms_b")]
    seg_mm, e_done, m_done, xdt_done, ctz_done = (sem(n) for n in ("seg_mm", "seg_exp", "m_done", "xdt_done", "c_groups_done"))
    off_mm, diag_mm, xd_done, gated = sem("y_off_mm"), sem("y_diag_mm"), sem("xd_done"), sem("y_gated")
    sq_done, rstd_done, normed, y_turned, mix_out = (sem(n) for n in ("y_sumsq", "y_rstd", "y_normed", "y_turned", "y_mix"))
    act_order, pool_turns = sem("ssd_act_order"), sem("ssd_pool_turns")
    heads = lambda t: t.rearrange("p (h e) -> p h e", h=NS)

    def terms(ops, eng, g, d):
        ops.tensor_tensor(r_sum[:, d], core.masks[:, (M_LE, M_GE)[d], :].unsqueeze(1).broadcast_to([P, NS, P]),
                          dta[:, bass.ds(g * 16 + 8 * d, 8)].unsqueeze(2).broadcast_to([P, NS, P]),
                          ALU.mult).then_inc(r_done[d], 1)

    with nc.Block() as block:
        @block.gpsimd
        def _(pool):
            def body(g, j, r):
                wait_apart(pool, seg_mm, g + 1, pool_turns)
                terms(nc.gpsimd, pool, g, 1)
                wait_apart(pool, diag_mm, g + 1, pool_turns)
                nc.gpsimd.tensor_tensor(xdt, heads(xnat[:, bass.ds(g * DSSD, DSSD)]).unsqueeze(1).broadcast_to([P, 2, NS, HP]),
                                        dt[:, bass.ds(g * 16, 16)].rearrange("p (d h) -> p d h", d=2).unsqueeze(3)
                                        .broadcast_to([P, 2, NS, HP]), ALU.mult).then_inc(xdt_done, 1)
                wait_apart(pool, gated, g + 1, pool_turns)
                nc.gpsimd.tensor_tensor(heads(y[:, 2]), heads(xnat[:, bass.ds(g * DSSD, DSSD)]),
                                        core.rows[:, ROW_D:ROW_D + 8].unsqueeze(2).broadcast_to([P, NS, HP]),
                                        ALU.mult).then_inc(xd_done, 1)
            tile_loop(pool, body)

        @block.scalar
        def _(act):
            act.preload_act_table_set("natural_log_exp_and_others")

            def body(g, j, r):
                act.wait_ge(seg_mm, g + 2)
                act.wait_ge(diag_mm, g + 1)
                for d in range(2):
                    for half in range(2):
                        nc.scalar.activation(e[:, d, 4 * half:4 * half + 4, :],
                                             core.ps[2 * d + half][:, :].rearrange("p (h q) -> p h q", h=4),
                                             ACT.Exp).then_inc(e_done, 1)
                act.wait_ge(gated, g + 2)
                for grp in range(2):
                    nc.scalar.activation(junk[:, 256 * grp:256 * grp + 256], y[:, 3, 256 * grp:256 * grp + 256],
                                         ACT.Square, accum_out=ss[:, grp:grp + 1]).then_inc(act_order, 1)
                act.wait_ge(act_order, g * 3 + 2)
                nc.scalar.activation(ln[:], ss[:], ACT.Ln, bias=core.eps[:, 0:1], scale=1.0 / 256).then_inc(act_order, 1)
                act.wait_ge(act_order, g * 3 + 3)
                nc.scalar.activation(rstd[:], ln[:], ACT.Exp, scale=-0.5).then_inc(rstd_done, 1)
                act.wait_ge(y_turned, g + 1)
                for c in range(4):
                    ins = nc.scalar.activation(mixT[:, 4 + c, bass.ds(g * P, P)], core.ps[7][:, c * P:(c + 1) * P],
                                               ACT.Copy, scale=core.col("ssd_norm", c))
                ins.then_inc(mix_out, 1)
            tile_loop(act, body)

        @block.vector
        def _(dve):
            dve.sem_inc(seg_mm, 1)
            dve.sem_inc(diag_mm, 1)
            dve.sem_inc(gated, 1)
            for t in ctz:
                nc.vector.memset(t[0:64, 1, :], 0.0)
                nc.vector.memset(t[64:128, 0, :], 0.0)

            def body(g, j, r):
                order = Order(dve, sem("ssd_dve_order"), g * 4)
                dve.wait_ge(seg_mm, g + 1)
                terms(nc.vector, dve, g, 0)
                nc.vector.tensor_copy(ctz[j][0:64, 0, :], ct[0:64, bass.ds(g * P, P)])
                nc.vector.tensor_copy(ctz[j][64:128, 1, :], ct[64:128, bass.ds(g * P, P)]).then_inc(ctz_done, 1)
                for d in range(2):
                    ins = nc.vector.tensor_tensor(
                        cbm[:, d], cb[:, bass.ds(g * 256, 256)].rearrange("p (a q) -> p a q", a=2),
                        core.masks[:, (M_LE, M_GE)[d], :].unsqueeze(1).broadcast_to([P, 2, P]), ALU.mult)
                order.link(ins)
                for d in range(2):
                    dve.wait_ge(e_done, g * 4 + (2 * d + 2))
                    v = e[:, d].rearrange("p (a h) q -> p a h q", a=2)
                    nc.vector.tensor_tensor(v, v, cbm[:, d].unsqueeze(2).broadcast_to([P, 2, 4, P]),
                                            ALU.mult).then_inc(m_done, 1)
                dve.wait_ge(off_mm, g + 1)
                for d in range(2):
                    nc.vector.tensor_tensor(
                        heads(y[:, d]), heads(core.ps[5 + d][:, :]),
                        dec[:, (D_CSF, D_CSB)[d], bass.ds(g * 16 + 8 * d, 8)].unsqueeze(2).broadcast_to([P, NS, HP]),
                        ALU.mult).then_inc(sem("y_off_done"), 1)
                dve.wait_ge(sem("y_off_done"), g * 2 + 2)
                order.link(nc.vector.tensor_tensor(y[:, 0], y[:, 0], y[:, 1], ALU.add))
                dve.wait_ge(xd_done, g + 1)
                order.link(nc.vector.tensor_tensor(y[:, 0], y[:, 0], y[:, 2], ALU.add))
                dve.wait_ge(diag_mm, g + 2)
                order.link(nc.vector.tensor_tensor(y[:, 0], y[:, 0], core.ps[4][:, :], ALU.add))
                nc.vector.tensor_tensor(y[:, 3], y[:, 0], z[:, bass.ds(g * DSSD, DSSD)], ALU.mult).then_inc(gated, 1)
                dve.wait_ge(rstd_done, g + 1)
                for grp in range(2):
                    ins = nc.vector.tensor_scalar(y[:, 4, 256 * grp:256 * grp + 256], y[:, 3, 256 * grp:256 * grp + 256],
                                                  rstd[:, grp:grp + 1], None, ALU.mult)
                ins.then_inc(normed, 1)
                assert order.n == 4
            tile_loop(dve, body)

        @block.tensor
        def _(pe):
            def body(g, j, r):
                for d in range(2):
                    pe.wait_ge(r_done[d], g + 1)
                    for half in range(2):
                        mm = nc.tensor.matmul(core.ps[2 * d + half][:, :], core.masks[:, (M_GT, M_LT)[d], :],
                                              r_sum[:, d, 4 * half:4 * half + 4, :].rearrange("p h q -> p (h q)"),
                                              start=True, stop=True)
                mm.then_inc(seg_mm, 1)
                pe.wait_ge(ctz_done, g + 1)
                for d in range(2):
                    for grp in range(2):
                        mm = nc.tensor.matmul(core.ps[5 + d][:, 256 * grp:256 * grp + 256], ctz[j][:, grp, :],
                                              st[d][:, bass.ds(slot_in(g, r, d), 256)], start=True, stop=True)
                mm.then_inc(off_mm, 1)
                pe.wait_ge(m_done, g * 2 + 2)
                pe.wait_ge(xdt_done, g + 1)
                for h in range(NS):
                    for d in range(2):
                        mm = nc.tensor.matmul(core.ps[4][:, h * HP:(h + 1) * HP], e[:, d, h, :], xdt[:, d, h, :],
                                              start=(d == 0), stop=(d == 1))
                mm.then_inc(diag_mm, 1)
                pe.wait_ge(normed, g + 1)
                for c in range(4):
                    mm = nc.tensor.transpose(core.ps[7][:, c * P:(c + 1) * P], y[:, 4, c * P:(c + 1) * P], core.ident)
                mm.then_inc(y_turned, 1)
            tile_loop(pe, body)


A_KT, A_WUQ, A_WUKV = 0, 8192, 9728
A_KN = 10752
A_V = A_DT
A_P, A_PT = A_V + 4096, A_V + 6144
A_QN, A_QT = A_V + 8192, A_V + 9728
A_O, A_CN, A_CT2 = A_V + 11776, A_V + 13824, A_V + 14592
A_ROT = A_V + 15360


def rope(nc, link, out1, out2, x1, x2, cos, sin, t):
    nc.vector.tensor_tensor(t[0], x1, cos, ALU.mult)
    nc.vector.tensor_tensor(t[1], x2, sin, ALU.mult)
    nc.vector.tensor_tensor(t[2], x2, cos, ALU.mult)
    link(nc.vector.tensor_tensor(t[3], x1, sin, ALU.mult))
    nc.vector.tensor_tensor(out1, t[0], t[1], ALU.subtract)
    return nc.vector.tensor_tensor(out2, t[2], t[3], ALU.add)


def keys(core, A, r):
    nc, io, sem = core.nc, core.io, core.sem
    lo, hi = TILES[r]
    nat = A.at(A_NAT, NT * NAT)
    kT = A.at(A_KT, NH, 1024)
    wuq, wukv = A.at(A_WUQ, 2, NH * DQK), A.at(A_WUKV, NH * (DN + DV))
    kn = [A.at(A_KN + 768 * j, NH, DQK) for j in range(2)]
    v = A.at(A_V, 4096)
    cn = [A.at(A_CN + 384 * j, 384) for j in range(2)]
    cT = [A.at(A_CT2 + 384 * j, 3, P) for j in range(2)]
    rot = [A.at(A_ROT + 16 * i, 16) for i in range(4)]
    ss, ln, rstd = (core.small(f"kv_{n}{r}", [P, 2]) for n in ("ss", "ln", "rstd"))
    junk = A.at(A_ROT + 64, P)
    order_a, rstd_done, cn_done = sem("kv_act_order"), sem("kv_rstd"), sem("ckv_normed")
    turned, cT_done, kv_mm, rot_order = sem("ckv_turned"), sem("ckvT_done"), sem("kv_mm"), sem("k_rot_order")
    kn_done, v_done, k_turned, kT_act, kT_dve = (sem(n) for n in ("kn_done", "v_done", "k_turned", "kT_act", "kT_dve"))

    def tiles(eng, body):
        with eng.Fori(0, (hi - lo) // 2) as turn:
            for j in range(2):
                body(turn * 2 + (lo + j), turn * 2 + j, j)

    with nc.Block() as block:
        if r == 0:
            @block.sync
            def _(sp):
                sp.dma_start(wuq, io["w_uq"][0].rearrange("(k p) n -> p k n", p=P)).then_inc(sem("w_qkv_in"), 16)
                sp.dma_start(wukv, io["w_ukv"][0]).then_inc(sem("w_qkv_in"), 16)

        @block.scalar
        def _(act):
            act.preload_act_table_set("natural_log_exp_and_others")

            def body(g, i, j):
                nc.scalar.activation(junk, nat[:, bass.ds(g * NAT + QL, KVL)], ACT.Square,
                                     accum_out=ss[:, j:j + 1]).then_inc(order_a, 1)
                act.wait_ge(order_a, g * 2 + 1)
                nc.scalar.activation(ln[:, j:j + 1], ss[:, j:j + 1], ACT.Ln, bias=core.eps[:, 0:1],
                                     scale=1.0 / KVL).then_inc(order_a, 1)
                act.wait_ge(order_a, g * 2 + 2)
                nc.scalar.activation(rstd[:, j:j + 1], ln[:, j:j + 1], ACT.Exp, scale=-0.5).then_inc(rstd_done, 1)
                act.wait_ge(turned, g + 1)
                nc.scalar.activation(cT[j][:, 2, :], core.ps[0][:, 0:P], ACT.Copy,
                                     scale=core.col("kv_norm")).then_inc(cT_done, 1)
                act.wait_ge(kv_mm, g + 1)
                kv = core.ps[1].rearrange("p (h e) -> p h e", h=4)
                nc.scalar.activation(kn[j][:, 0:4, 0:DN], kv[:, :, 0:DN], ACT.Copy)
                nc.scalar.activation(v[:, bass.ds(i * 512, 256)].rearrange("p (h e) -> p h e", h=4), kv[:, :, DN:],
                                     ACT.Copy).then_inc(v_done, 1)
                act.wait_ge(k_turned, g + 1)
                nc.scalar.activation(kT[0:DQK, 0:4, bass.ds(i * P, P)],
                                     core.ps[3][0:DQK, :].rearrange("p (h t) -> p h t", h=4), ACT.Copy).then_inc(kT_act, 1)
            tiles(act, body)

        @block.vector
        def _(dve):
            def body(g, i, j):
                order = Order(dve, rot_order, g)
                dve.wait_ge(rstd_done, g + 1)
                nc.vector.tensor_scalar(cn[j][:, QL:], nat[:, bass.ds(g * NAT + QL, KVL)], rstd[:, j:j + 1], None,
                                        ALU.mult).then_inc(cn_done, 1)
                kr = nat[:, bass.ds(g * NAT + (QL + KVL), DR)]
                ropes = core.rope[:, bass.ds(i, 1)].rearrange("p o s f -> p (o s f)")
                spread = [t.unsqueeze(1).broadcast_to([P, NH, 16]) for t in rot]
                nc.vector.tensor_tensor(rot[0], kr[:, 0:16], ropes[:, 0:16], ALU.mult)
                nc.vector.tensor_tensor(rot[1], kr[:, 16:32], ropes[:, 16:32], ALU.mult)
                nc.vector.tensor_tensor(rot[2], kr[:, 16:32], ropes[:, 0:16], ALU.mult)
                order.link(nc.vector.tensor_tensor(rot[3], kr[:, 0:16], ropes[:, 16:32], ALU.mult))
                nc.vector.tensor_tensor(kn[j][:, :, DN:DN + 16], spread[0], spread[1], ALU.subtract)
                nc.vector.tensor_tensor(kn[j][:, :, DN + 16:], spread[2], spread[3], ALU.add)
                dve.wait_ge(kv_mm, g + 1)
                kv = core.ps[2].rearrange("p (h e) -> p h e", h=4)
                nc.vector.tensor_copy(kn[j][:, 4:8, 0:DN], kv[:, :, 0:DN])
                nc.vector.tensor_copy(v[:, bass.ds(i * 512 + 256, 256)].rearrange("p (h e) -> p h e", h=4),
                                      kv[:, :, DN:]).then_inc(kn_done, 1)
                dve.wait_ge(k_turned, g + 1)
                nc.vector.tensor_copy(kT[0:DQK, 4:8, bass.ds(i * P, P)],
                                      core.ps[4][0:DQK, :].rearrange("p (h t) -> p h t", h=4)).then_inc(kT_dve, 1)
            tiles(dve, body)

        @block.tensor
        def _(pe):
            pe.wait_ge(sem("w_qkv_in"), 32)

            def body(g, i, j):
                pe.wait_ge(cn_done, g + 1)
                nc.tensor.transpose(core.ps[0][:, 0:P], cn[j][:, QL:], core.ident).then_inc(turned, 1)
                pe.wait_ge(cT_done, g + 1)
                for half in range(2):
                    mm = nc.tensor.matmul(core.ps[1 + half], cT[j][:, 2, :], wukv[:, 512 * half:512 * half + 512],
                                          start=True, stop=True)
                mm.then_inc(kv_mm, 1)
                pe.wait_ge(kn_done, g + 1)
                pe.wait_ge(v_done, g + 1)
                for h in range(NH):
                    mm = nc.tensor.transpose(core.ps[3 + h // 4][0:DQK, h % 4 * P:(h % 4 + 1) * P], kn[j][:, h, :],
                                             core.ident)
                mm.then_inc(k_turned, 1)
            tiles(pe, body)


Q_STATS, Q_TURN, Q_MM0, Q_MM1, Q_ROPE, Q_T0, Q_T1 = range(7)


def attention(core, A, r):
    nc, io, sem = core.nc, core.io, core.sem
    lo, hi = TILES[r]
    n_tiles = hi - lo
    keys_n = T_OF[r]
    nkt = keys_n // P
    nat = A.at(A_NAT, NT * NAT)
    kT = A.at(A_KT, NH, 1024)
    wuq = A.at(A_WUQ, 2, NH * DQK)
    v = A.at(A_V, 8, NH, DV)
    prob = [A.at(A_P + 1024 * b, 1024) for b in range(2)]
    probT = [A.at(A_PT + 1024 * b, 8, P) for b in range(2)]
    qn = [A.at(A_QN + 768 * j, NH, DQK) for j in range(2)]
    qT = [A.at(A_QT + 1024 * j, NH, P) for j in range(2)]
    o = [A.at(A_O + 1024 * j, 2, NH * DV) for j in range(2)]
    cn = [A.at(A_CN + 384 * j, 384) for j in range(2)]
    cT = [A.at(A_CT2 + 384 * j, 3, P) for j in range(2)]
    rot = [A.at(A_ROT + P * i, NH, 16) for i in range(4)]
    mixT = A.at(A_MIX, 8, NT * P)
    junk = A.at(A_ROT + 4 * P, 512)
    q_ss, q_ln, q_rstd, o_ss, o_ln, o_rstd, top, bias = (
        core.small(f"att_{n}{r}", [P, 2]) for n in ("q_ss", "q_ln", "q_rstd", "o_ss", "o_ln", "o_rstd", "top", "bias"))
    total = core.small(f"att_total{r}", [P, 2, NH])
    inv = core.small(f"att_inv{r}", [P, 2, NH])
    q_rstd_done, cq_normed, cq_turned, cqT_done, q_mm, q_copied, q_roped, q_turned, qT_done = (
        sem(n) for n in ("q_rstd", "cq_normed", "cq_turned", "cqT_done", "q_mm", "q_copied", "q_roped", "q_turned", "qT_done"))
    scored, topped, biased, exped, p_turned, pT_act, pT_dve, valued = (
        sem(n) for n in ("scored", "topped", "biased", "exped", "p_turned", "pT_act", "pT_dve", "valued"))
    o_done, o_rstd_done, o_normed, o_turned, o_mixed = (
        sem(n) for n in ("o_done", "o_rstd", "o_normed", "o_turned", "o_mixed"))
    act_order, o_order, dve_order, inv_done = sem("att_act_order"), sem("att_o_order"), sem("att_dve_order"), sem("att_inv")
    half = nkt // 2
    spare = core.ps[7]

    def tiles(eng, first, body):
        first()
        if n_tiles > 2:
            with eng.Fori(0, n_tiles // 2 - 1) as turn:
                for j in range(2):
                    body(turn * 2 + (lo + j), turn * 2 + j, j, True)
        for j in range(2):
            body(hi - 2 + j, n_tiles - 2 + j, j, j == 0)

    with nc.Block() as block:
        @block.scalar
        def _(act):
            act.preload_act_table_set("natural_log_exp_and_others")

            def front(step, g, i, j):
                if step == Q_STATS:
                    nc.scalar.activation(junk[:, 0:QL], nat[:, bass.ds(g * NAT, QL)], ACT.Square,
                                         accum_out=q_ss[:, j:j + 1]).then_inc(act_order, 1)
                    act.wait_ge(act_order, g * 2 + 1)
                    nc.scalar.activation(q_ln[:, j:j + 1], q_ss[:, j:j + 1], ACT.Ln, bias=core.eps[:, 0:1],
                                         scale=1.0 / QL).then_inc(act_order, 1)
                    act.wait_ge(act_order, g * 2 + 2)
                    nc.scalar.activation(q_rstd[:, j:j + 1], q_ln[:, j:j + 1], ACT.Exp, scale=-0.5).then_inc(q_rstd_done, 1)
                elif step == Q_TURN:
                    act.wait_ge(cq_turned, g + 1)
                    for k in range(2):
                        ins = nc.scalar.activation(cT[j][:, k, :], spare[:, k * P:(k + 1) * P], ACT.Copy,
                                                   scale=core.col("q_norm", k))
                    ins.then_inc(cqT_done, 1)
                elif step in (Q_MM0, Q_MM1):
                    part, h0, h1 = (0, 0, 5) if step == Q_MM0 else (1, 5, 8)
                    act.wait_ge(q_mm, g * 2 + (part + 1))
                    nc.scalar.activation(qn[j][:, h0:h1, :].rearrange("p h e -> p (h e)"),
                                         spare[:, 0:(h1 - h0) * DQK], ACT.Copy).then_inc(q_copied, 1)

            def exps(g, h, j):
                act.wait_ge(biased, g * NH + (h + 1))
                nc.scalar.activation(prob[h % 2][:, 0:keys_n], core.banks[:, h % 2 * 1024:h % 2 * 1024 + keys_n],
                                     ACT.Exp, bias=bias[:, h % 2:h % 2 + 1], scale=SCALE,
                                     accum_out=total[:, j, h:h + 1]).then_inc(exped, 1)

            def first():
                for step in range(7):
                    front(step, lo, 0, 0)
                exps(lo, 0, 0)

            def body(g, i, j, more):
                for h in range(NH):
                    if h + 1 < NH:
                        exps(g, h + 1, j)
                    elif more:
                        exps(g + 1, 0, 1 - j)
                    act.wait_ge(p_turned, g * NH + (h + 1))
                    nc.scalar.activation(probT[h % 2][:, 0:half, :],
                                         core.banks[:, 2048:2048 + half * P].rearrange("p (k q) -> p k q", k=half),
                                         ACT.Copy).then_inc(pT_act, 1)
                    if more and h < 7:
                        front(h, g + 1, i + 1, 1 - j)
                act.wait_ge(o_done, g + 2)
                nc.scalar.activation(junk, o[j][:, 0, :], ACT.Square, accum_out=o_ss[:, j:j + 1]).then_inc(o_order, 1)
                act.wait_ge(o_order, g * 2 + 1)
                nc.scalar.activation(o_ln[:, j:j + 1], o_ss[:, j:j + 1], ACT.Ln, bias=core.eps[:, 0:1],
                                     scale=1.0 / (NH * DV)).then_inc(o_order, 1)
                act.wait_ge(o_order, g * 2 + 2)
                nc.scalar.activation(o_rstd[:, j:j + 1], o_ln[:, j:j + 1], ACT.Exp, scale=-0.5).then_inc(o_rstd_done, 1)
                act.wait_ge(o_turned, g + 1)
                for c in range(4):
                    ins = nc.scalar.activation(mixT[:, c, bass.ds(g * P, P)], spare[:, c * P:(c + 1) * P], ACT.Copy,
                                               scale=core.col("attn_norm", c))
                ins.then_inc(o_mixed, 1)
            tiles(act, first, body)

        @block.vector
        def _(dve):
            def front(step, g, i, j):
                if step == Q_STATS:
                    dve.wait_ge(q_rstd_done, g + 1)
                    nc.vector.tensor_scalar(cn[j][:, 0:QL], nat[:, bass.ds(g * NAT, QL)], q_rstd[:, j:j + 1], None,
                                            ALU.mult).then_inc(cq_normed, 1)
                elif step == Q_ROPE:
                    order = Order(dve, dve_order, g)
                    dve.wait_ge(q_copied, g * 2 + 2)
                    ropes = core.rope[:, bass.ds(i, 1)].rearrange("p o s f -> p (o s) f")
                    cos, sin = (ropes[:, s:s + 1, :].broadcast_to([P, NH, 16]) for s in range(2))
                    x1, x2 = qn[j][:, :, DN:DN + 16], qn[j][:, :, DN + 16:]
                    rope(nc, order.link, x1, x2, x1, x2, cos, sin, rot).then_inc(q_roped, 1)
                elif step in (Q_T0, Q_T1):
                    part = step - Q_T0
                    dve.wait_ge(q_turned, g * 2 + (part + 1))
                    nc.vector.tensor_copy(qT[j][0:DQK, 4 * part:4 * part + 4, :],
                                          spare[0:DQK, :].rearrange("p (h t) -> p h t", h=4)).then_inc(qT_done, 1)

            def tops(g, h):
                dve.wait_ge(scored, g * NH + (h + 1))
                nc.vector.tensor_reduce(top[:, h % 2:h % 2 + 1], core.banks[:, h % 2 * 1024:h % 2 * 1024 + keys_n],
                                        AX_X, ALU.max).then_inc(topped, 1)
                dve.wait_ge(topped, g * NH + (h + 1))
                nc.vector.tensor_scalar(bias[:, h % 2:h % 2 + 1], top[:, h % 2:h % 2 + 1], -SCALE, None,
                                        ALU.mult).then_inc(biased, 1)

            def first():
                if r == 0:
                    dve.sem_inc(pT_dve, 1)
                    dve.sem_inc(pT_act, 1)
                    dve.sem_inc(o_done, 1)
                for step in range(7):
                    front(step, lo, 0, 0)
                tops(lo, 0)

            def body(g, i, j, more):
                for h in range(NH):
                    if h + 1 < NH:
                        tops(g, h + 1)
                    elif more:
                        tops(g + 1, 0)
                    dve.wait_ge(p_turned, g * NH + (h + 1))
                    nc.vector.tensor_copy(probT[h % 2][:, half:nkt, :],
                                          core.banks[:, 2560:2560 + half * P].rearrange("p (k q) -> p k q", k=half)
                                          ).then_inc(pT_dve, 1)
                    if more and h < 7:
                        front(h, g + 1, i + 1, 1 - j)
                dve.wait_ge(valued, g + 1)
                nc.vector.reciprocal(inv[:, j], total[:, j]).then_inc(inv_done, 1)
                dve.wait_ge(inv_done, g + 1)
                nc.vector.tensor_tensor(o[j][:, 0].rearrange("p (h e) -> p h e", h=NH),
                                        core.ps[6].rearrange("p (h e) -> p h e", h=NH),
                                        inv[:, j].unsqueeze(2).broadcast_to([P, NH, DV]), ALU.mult).then_inc(o_done, 1)
                dve.wait_ge(o_rstd_done, g + 1)
                nc.vector.tensor_scalar(o[j][:, 1], o[j][:, 0], o_rstd[:, j:j + 1], None, ALU.mult).then_inc(o_normed, 1)
            tiles(dve, first, body)

        @block.tensor
        def _(pe):
            def front(step, g, i, j):
                if step == Q_TURN:
                    pe.wait_ge(cq_normed, g + 1)
                    for k in range(2):
                        mm = nc.tensor.transpose(spare[:, k * P:(k + 1) * P], cn[j][:, k * P:(k + 1) * P], core.ident)
                    mm.then_inc(cq_turned, 1)
                elif step in (Q_MM0, Q_MM1):
                    part, h0, h1 = (0, 0, 5) if step == Q_MM0 else (1, 5, 8)
                    if part:
                        pe.wait_ge(q_copied, g * 2 + 1)
                    else:
                        pe.wait_ge(cqT_done, g + 1)
                    for k in range(2):
                        mm = nc.tensor.matmul(spare[:, 0:(h1 - h0) * DQK], cT[j][:, k, :],
                                              wuq[:, k, h0 * DQK:h1 * DQK], start=(k == 0), stop=(k == 1))
                    mm.then_inc(q_mm, 1)
                elif step in (Q_T0, Q_T1):
                    part = step - Q_T0
                    if part:
                        pe.wait_ge(qT_done, g * 2 + 1)
                    else:
                        pe.wait_ge(q_roped, g + 1)
                    for h in range(4):
                        mm = nc.tensor.transpose(spare[0:DQK, h * P:(h + 1) * P], qn[j][:, 4 * part + h, :], core.ident)
                    mm.then_inc(q_turned, 1)

            def scores(g, h, j):
                pe.wait_ge(qT_done, g * 2 + 2)
                for k0 in range(0, keys_n, 512):
                    mm = nc.tensor.matmul(core.banks[:, h % 2 * 1024 + k0:h % 2 * 1024 + k0 + 512],
                                          qT[j][0:DQK, h, :], kT[0:DQK, h, k0:k0 + 512], start=True, stop=True)
                mm.then_inc(scored, 1)

            def values(g, h):
                for k in range(nkt):
                    mm = nc.tensor.matmul(core.ps[6][:, h * DV:(h + 1) * DV], probT[h % 2][:, k, :], v[:, k, h, :],
                                          start=(k == 0), stop=(k == nkt - 1))
                return mm

            def first():
                for step in range(7):
                    front(step, lo, 0, 0)
                scores(lo, 0, 0)

            def body(g, i, j, more):
                for h in range(NH):
                    if h + 1 < NH:
                        scores(g, h + 1, j)
                    elif more:
                        scores(g + 1, 0, 1 - j)
                    pe.wait_ge(exped, g * NH + (h + 1))
                    pe.wait_ge(pT_act, g * NH + (h + 1))
                    pe.wait_ge(pT_dve, g * NH + (h + 1))
                    for k in range(nkt):
                        at = 2048 + 512 * (k // half) + k % half * P
                        mm = nc.tensor.transpose(core.banks[:, at:at + P],
                                                 prob[h % 2][:, k * P:(k + 1) * P], core.ident)
                    mm.then_inc(p_turned, 1)
                    if h == 1:
                        pe.wait_ge(o_done, g + 1)
                    if h:
                        values(g, h - 1)
                    if more and h < 7:
                        front(h, g + 1, i + 1, 1 - j)
                pe.wait_ge(pT_act, g * NH + (NH + 1))
                pe.wait_ge(pT_dve, g * NH + (NH + 1))
                values(g, NH - 1).then_inc(valued, 1)
                pe.wait_ge(o_normed, g + 1)
                for c in range(4):
                    mm = nc.tensor.transpose(spare[:, c * P:(c + 1) * P], o[j][:, 1, c * P:(c + 1) * P], core.ident)
                mm.then_inc(o_turned, 1)
            tiles(pe, first, body)


def attend(core, A):
    for r in range(2):
        keys(core, A, r)
        attention(core, A, r)


A_WO, A_MT, A_WR = 0, 8192, 10240
A_OX = A_DT
A_GROW = A_OX + 9216
A_AFF = A_GROW + 2048


def row_of(nc, bank, columns, k, request, ident):
    return nc.tensor.matmul(bank[:, k % 4 * P:(k % 4 + 1) * P], columns.broadcast_to([P, P]), ident,
                            start=True, stop=True)


def output(core, A):
    nc, io, sem = core.nc, core.io, core.sem
    mixT = A.at(A_MIX, 8, NT * P)
    wo, wr = A.at(A_WO, 8, D), A.at(A_WR, KD, NE)
    mt = [A.at(A_MT + D * j, 8, P) for j in range(2)]
    x, x2, xn = ([A.at(A_OX + D * (2 * b + j), D) for j in range(2)] for b in range(3))
    hT = [A.at(A_OX + D * (6 + j), KD, P) for j in range(2)]
    junk = A.at(A_OX + 8 * D, D)
    gate_row = A.at(A_GROW, 2, D)
    aff = core.aff = A.at(A_AFF, 1024)
    ss, ln, rstd, top, total, inv = (core.small(f"out_{n}", [P, 2]) for n in ("ss", "ln", "rstd", "top", "total", "inv"))
    soft = [core.small(f"soft_aff{j}", [P, 2, NE]) for j in range(2)]
    x_in = [sem(f"out_x_in{j}") for j in range(2)]
    res_out, normed_out = ([sem(f"{n}{j}") for j in range(2)] for n in ("residual_out", "normed_out"))
    rows_mm, rows_done, mt_done, proj_mm, gated, x2_done = (
        sem(n) for n in ("gate_rows_mm", "gate_rows", "mt_done", "out_mm", "out_gated", "x2_done"))
    act_order, rstd_done, xn_done, turned, hT_act, hT_dve = (
        sem(n) for n in ("out_act_order", "out_rstd", "out_xn", "out_turned", "h2T_act", "h2T_dve"))
    logits, topped, exped, inv_done, soft_done, aff_turned, aff_done = (
        sem(n) for n in ("logits", "logit_top", "logit_exp", "logit_inv", "soft_done", "aff_turned", "aff_done"))
    x_of = (io["x_prompt"], io["x_sample"])

    with nc.Block() as block:
        @block.sync
        def _(sp):
            sp.dma_start(wo, io["w_out"][0].rearrange("(k p) n -> p k n", p=P)).then_inc(sem("w_out_in"), 16)
            sp.dma_start(wr, io["w_router"][0].rearrange("(k p) n -> p k n", p=P)).then_inc(sem("w_out_in"), 16)

            def front(g, j, r):
                sp.wait_ge(x2_done, g + 1)
                load_tile(sp, x[j], x_of, g, r, x_in[j])

            def back(g, j, r):
                sp.wait_ge(x2_done, g + 3)
                sp.dma_start(core.residual[bass.ds(g * P, P), :], x2[j]).then_inc(res_out[j], 16)
                sp.wait_ge(xn_done, g + 1)
                sp.dma_start(core.normed[bass.ds(g * P, P), :], xn[j]).then_inc(normed_out[j], 16)
            tile_loop_ahead(sp, front, back)
            for j in range(2):
                sp.wait_ge(res_out[j], NT // 2 * 16)
                sp.wait_ge(normed_out[j], NT // 2 * 16)

        @block.scalar
        def _(act):
            act.preload_act_table_set("natural_log_exp_and_others")

            def front(g, j, r):
                act.wait_ge(x2_done, g + 3)
                nc.scalar.activation(junk, x2[j], ACT.Square, accum_out=ss[:, j:j + 1]).then_inc(act_order, 1)
                act.wait_ge(act_order, g * 2 + 1)
                nc.scalar.activation(ln[:, j:j + 1], ss[:, j:j + 1], ACT.Ln, bias=core.eps[:, 0:1],
                                     scale=1.0 / D).then_inc(act_order, 1)
                act.wait_ge(act_order, g * 2 + 2)
                nc.scalar.activation(rstd[:, j:j + 1], ln[:, j:j + 1], ACT.Exp, scale=-0.5).then_inc(rstd_done, 1)

            def back(g, j, r):
                act.wait_ge(turned, g + 1)
                for k in range(4):
                    ins = nc.scalar.activation(hT[j][:, k, :], core.ps[2][:, k * P:(k + 1) * P], ACT.Identity,
                                               bias=core.mod[:, 3 * KD + k, r:r + 1], scale=core.scale2[:, k, r:r + 1])
                ins.then_inc(hT_act, 1)
                act.wait_ge(topped, g * 2 + 2)
                nc.scalar.activation(soft[j][:, 0], core.ps[4][:, 0:NE], ACT.Exp, bias=top[:, j:j + 1],
                                     accum_out=total[:, j:j + 1]).then_inc(exped, 1)
            tile_loop_ahead(act, front, back)

        @block.vector
        def _(dve):
            dve.sem_inc(x2_done, 2)
            nc.vector.memset(aff[0:48, :], -1.0)
            for r in range(2):
                for half in range(2):
                    dve.wait_ge(rows_mm, 2 * r + half + 1)
                    nc.vector.tensor_copy(gate_row[:, r, 512 * half:512 * half + 512], core.ps[half]).then_inc(rows_done, 1)

            def front(g, j, r):
                nc.vector.tensor_copy(mt[j], mixT[:, :, bass.ds(g * P, P)]).then_inc(mt_done, 1)
                if isinstance(g, int) and g == 0:
                    dve.wait_ge(rows_done, 4)
                if isinstance(g, int) and g < 2:
                    pass
                else:
                    dve.wait_ge(res_out[j], (g - j) * 8)
                dve.wait_ge(proj_mm, g + 1)
                for half in range(2):
                    ins = nc.vector.tensor_tensor(x2[j][:, 512 * half:512 * half + 512], core.ps[half],
                                                  gate_row[:, r, 512 * half:512 * half + 512], ALU.mult)
                ins.then_inc(gated, 1)
                dve.wait_ge(x_in[j], (g - j) * 8 + 16)
                dve.wait_ge(gated, g + 1)
                nc.vector.tensor_tensor(x2[j], x2[j], x[j], ALU.add).then_inc(x2_done, 1)
                dve.wait_ge(rstd_done, g + 1)
                if isinstance(g, int) and g < 2:
                    pass
                else:
                    wait_apart(dve, normed_out[j], (g - j) * 8, sem("out_dve_turns"))
                nc.vector.tensor_scalar(xn[j], x2[j], rstd[:, j:j + 1], None, ALU.mult).then_inc(xn_done, 1)

            def back(g, j, r):
                dve.wait_ge(turned, g + 1)
                for k in range(4, KD):
                    ins = nc.vector.tensor_scalar(hT[j][:, k, :], core.ps[3][:, (k - 4) * P:(k - 3) * P],
                                                  core.scale2[:, k, r:r + 1], core.mod[:, 3 * KD + k, r:r + 1],
                                                  ALU.mult, ALU.add)
                ins.then_inc(hT_dve, 1)
                dve.wait_ge(logits, g + 1)
                nc.vector.tensor_reduce(inv[:, j:j + 1], core.ps[4][:, 0:NE], AX_X, ALU.max).then_inc(topped, 1)
                dve.wait_ge(topped, g * 2 + 1)
                nc.vector.tensor_scalar(top[:, j:j + 1], inv[:, j:j + 1], -1.0, None, ALU.mult).then_inc(topped, 1)
                dve.wait_ge(exped, g + 1)
                nc.vector.reciprocal(inv[:, j:j + 1], total[:, j:j + 1]).then_inc(inv_done, 1)
                dve.wait_ge(inv_done, g + 1)
                nc.vector.tensor_scalar(soft[j][:, 1], soft[j][:, 0], inv[:, j:j + 1], None, ALU.mult).then_inc(soft_done, 1)
                dve.wait_ge(aff_turned, g + 1)
                nc.vector.tensor_copy(aff[32 * r:32 * r + NE, bass.ds((g - TILES[r][0]) * P, P)],
                                      core.ps[5][0:NE, 0:P]).then_inc(aff_done, 1)
            tile_loop_ahead(dve, front, back)

        @block.tensor
        def _(pe):
            for r in range(2):
                for half in range(2):
                    if r:
                        pe.wait_ge(rows_done, half + 1)
                    for k in range(4 * half, 4 * half + 4):
                        mm = row_of(nc, core.ps[half], core.mod[:, 2 * KD + k, r:r + 1], k, r, core.ident)
                    mm.then_inc(rows_mm, 1)
            pe.wait_ge(sem("w_out_in"), 32)
            pe.wait_ge(rows_done, 4)

            def front(g, j, r):
                pe.wait_ge(mt_done, g + 1)
                pe.wait_ge(x2_done, g + 2)
                for half in range(2):
                    for k in range(8):
                        mm = nc.tensor.matmul(core.ps[half], mt[j][:, k, :], wo[:, k, 512 * half:512 * half + 512],
                                              start=(k == 0), stop=(k == 7))
                mm.then_inc(proj_mm, 1)

            def back(g, j, r):
                pe.wait_ge(xn_done, g + 1)
                for k in range(KD):
                    mm = nc.tensor.transpose(core.ps[2 + k // 4][:, k % 4 * P:(k % 4 + 1) * P],
                                             xn[j][:, k * P:(k + 1) * P], core.ident)
                mm.then_inc(turned, 1)
                pe.wait_ge(hT_act, g + 1)
                pe.wait_ge(hT_dve, g + 1)
                for k in range(KD):
                    mm = nc.tensor.matmul(core.ps[4][:, 0:NE], hT[j][:, k, :], wr[:, k, :],
                                          start=(k == 0), stop=(k == KD - 1))
                mm.then_inc(logits, 1)
                pe.wait_ge(soft_done, g + 1)
                nc.tensor.transpose(core.ps[5][0:NE, 0:P], soft[j][:, 1], core.ident).then_inc(aff_turned, 1)
            tile_loop_ahead(pe, front, back)


def choice(core, A):
    nc, sem = core.nc, core.sem
    left = [A.at(A_AFF, 1024)[0:48, :], A.at(0, 1024)[0:48, :]]
    best = A.at(1024, CAP[1])[0:48, :]
    place = A.at(1152, CAP[1])[0:48, :]
    places = core.small("places", [48, CAP[1]], U32)
    ranked, turned = sem("choice_order"), sem("choice_turned")

    with nc.Block() as block:
        @block.vector
        def _(dve):
            order = Order(dve, ranked)
            for n in range(CAP[1] // 8):
                eight = slice(8 * n, 8 * n + 8)
                now, then = left[n % 2], left[1 - n % 2]
                order.link(nc.vector.max(best[:, eight], now))
                nc.vector.max_index(places[:, eight], best[:, eight], now)
                order.link(nc.vector.match_replace(then, best[:, eight], now, -2.0))
            nc.vector.tensor_copy(place[0:32], places[0:32, :])
            order.link(nc.vector.tensor_scalar(place[32:48], places[32:48, :], float(T_OF[0]), None, ALU.add))
            dve.sem_inc(sem("choice_ready"), 1)
            dve.wait_ge(turned, 1)
            nc.vector.tensor_copy(core.chosen[:], core.ps[0][:, 0:48])
            nc.vector.tensor_copy(core.gates[:], core.ps[0][:, 64:112])

        @block.tensor
        def _(pe):
            pe.wait_ge(sem("choice_ready"), 1)
            nc.tensor.transpose(core.ps[0][:, 0:48], place, core.ident[0:48, 0:48])
            nc.tensor.transpose(core.ps[0][:, 64:112], best, core.ident[0:48, 0:48]).then_inc(turned, 1)


SLAB = KD * 512
E_X, E_XT, E_HID = 6 * SLAB, 6 * SLAB + 2 * D, 6 * SLAB + 2 * D + 1536
E_YT = E_HID + 1536
E_Y = E_YT + 1536
E_SIL = E_Y + 2 * D
CT = sum(CAP)
SPLIT = ((1, 0, CAP[1]), (0, CAP[1], CT))
FS = FE // 512


def experts(core, A):
    nc, io, sem = core.nc, core.io, core.sem
    slab = [[A.at(SLAB * (3 * s + kind), *((4, D) if kind == 2 else (KD, 512))) for kind in range(3)] for s in range(2)]
    xe = [A.at(E_X + D * b, D)[0:CAP[r]] for b, r in enumerate((1, 0))]
    xT, yT = A.at(E_XT, KD, CT), A.at(E_YT, KD, CT)
    hid = [A.at(E_HID + 768 * b, 4, CT) for b in range(2)]
    y = [A.at(E_Y + D * b, D)[0:CAP[r]] for b, r in enumerate((1, 0))]
    sil = [A.at(E_SIL + CT * b, CT) for b in range(2)]
    rows_in = [core.small(f"rows_in{b}", [CAP[r], 1], U32) for b, r in enumerate((1, 0))]
    rows_out = [core.small(f"rows_out{b}", [CAP[r], 1], U32) for b, r in enumerate((1, 0))]
    slab_in = [[sem(f"slab{s}_{kind}_in") for kind in ("gate", "up", "down")] for s in range(2)]
    down_used = sem("slab_down_used")
    xe_in, y_out = ([sem(f"{n}{b}") for b in range(2)] for n in ("xe_in", "y_scattered"))
    rows_copied = sem("rows_copied")
    x_turned, xT_act, xT_dve = sem("xe_turned"), sem("xeT_act"), sem("xeT_dve")
    gu_mm, sil_done, hid_done = sem("gate_up_mm"), sem("silu_gate"), sem("hid_done")
    yT_act, yT_dve, y_turned, y_act, y_dve = (sem(n) for n in ("yT_act", "yT_dve", "y_e_turned", "y_e_act", "y_e_dve"))
    y_banks = core.banks[:, 1024:3072].rearrange("p (b c) -> p b c", c=512)

    def y_part(dc):
        return y_banks[:, dc // 2, 256 * (dc % 2):256 * (dc % 2) + CT]

    with nc.Block() as block:
        @block.sync
        def _(sp):
            views = (io["w_gate"][0].rearrange("e (k p) n -> p e k n", p=P),
                     io["w_up"][0].rearrange("e (k p) n -> p e k n", p=P),
                     io["w_down"][0].rearrange("e (k p) n -> p e k n", p=P))

            def load(e, fs, first):
                s = fs % 2
                for kind in range(3):
                    if not first:
                        if kind == 0:
                            sp.wait_ge(gu_mm, e * 16 + 4 * (fs - 1))
                        elif kind == 2:
                            sp.wait_ge(down_used, e * FS + (fs - 1))
                    src = views[kind][:, bass.ds(e, 1)] if not isinstance(e, int) else views[kind][:, e:e + 1]
                    src = src[:, :, 4 * fs:4 * fs + 4, :] if kind == 2 else src[:, :, :, 512 * fs:512 * fs + 512]
                    sp.dma_start(slab[s][kind], src.rearrange("p e k n -> p (e k) n")).then_inc(slab_in[s][kind], 16)
            for fs in range(FS):
                load(0, fs, fs < 2)
            with sp.Fori(1, NE) as e:
                for fs in range(FS):
                    load(e, fs, False)

        @block.gpsimd
        def _(pool):
            def gather(e):
                for b, (r, _, _) in enumerate(SPLIT):
                    nc.gpsimd.tensor_copy(rows_in[b][:], core.chosen[0:CAP[r], bass.ds(e + 32 * r, 1)]).then_inc(rows_copied, 1)
                copies = 2 if isinstance(e, int) and e == 0 else e * 4
                wait_apart(pool, rows_copied, copies, sem("experts_pool_turns"))
                for b in range(2):
                    nc.gpsimd.indirect_dma_start(xe[b], None, core.normed, bass.IndirectOffsetOnAxis(ap=rows_in[b][:, 0:1], axis=0)
                                                 ).then_inc(xe_in[b], 16)

            def scatter(e):
                if not (isinstance(e, int) and e == 0):
                    for b in range(2):
                        wait_apart(pool, y_out[b], e * 16, sem("experts_pool_turns"))
                for b, (r, _, _) in enumerate(SPLIT):
                    ins = nc.gpsimd.tensor_copy(rows_out[b][:], core.chosen[0:CAP[r], bass.ds(e + 32 * r, 1)])
                    ins.then_inc(rows_copied, 1)
                pool.wait_ge(rows_copied, e * 4 + 6 if not (isinstance(e, int) and e == NE - 1) else 4 * NE)
                for b in range(2):
                    pool.wait_ge(y_act, e * 2 + (b + 1))
                    wait_apart(pool, y_dve, e * 2 + (b + 1), sem("experts_pool_turns"))
                    nc.gpsimd.indirect_dma_start(core.residual, bass.IndirectOffsetOnAxis(ap=rows_out[b][:, 0:1], axis=0),
                                                 y[b], None, compute_op=ALU.add).then_inc(y_out[b], 16)

            def turn(e, more):
                if more:
                    wait_apart(pool, x_turned, e * 2 + 2, sem("experts_pool_turns"))
                    gather(e + 1)
                scatter(e)
            gather(0)
            turn(0, True)
            with pool.Fori(1, NE - 1) as e:
                turn(e, True)
            turn(NE - 1, False)
            for b in range(2):
                pool.wait_ge(y_out[b], NE * 16)

        def evacuate(eng, chunk, dst, src, scale, bias):
            if chunk < 4:
                if bias is None:
                    return nc.scalar.activation(dst, src, ACT.Copy, scale=scale)
                return nc.scalar.activation(dst, src, ACT.Identity, scale=scale, bias=bias)
            if bias is None:
                return nc.vector.tensor_scalar(dst, src, scale, None, ALU.mult)
            return nc.vector.tensor_scalar(dst, src, scale, bias, ALU.mult, ALU.add)

        def drain_x(eng, chunks, e, b, done):
            r, c0, c1 = SPLIT[b]
            eng.wait_ge(x_turned, e * 2 + (b + 1))
            for k in chunks:
                ins = evacuate(eng, k, xT[:, k, c0:c1], core.ps[6 + k // 4][:, k % 4 * P:k % 4 * P + c1 - c0],
                               core.scale2[:, k, r:r + 1], core.mod[:, 3 * KD + k, r:r + 1])
            ins.then_inc(done, 1)

        def drain_yT(eng, chunks, e, done):
            eng.wait_ge(down_used, e * FS + FS)
            for dc in chunks:
                for r, c0, c1 in SPLIT:
                    ins = evacuate(eng, dc, yT[:, dc, c0:c1], y_part(dc)[:, c0:c1], core.mod[:, 5 * KD + dc, r:r + 1], None)
            ins.then_inc(done, 1)

        def drain_y(eng, half, e, b, done):
            r, c0, c1 = SPLIT[b]
            n = CAP[r]
            eng.wait_ge(y_turned, e * 2 + (b + 1))
            gate = core.gates[0:n, bass.ds(e + 32 * r, 1)]
            evacuate(eng, 4 * half, y[b][:, 512 * half:512 * half + 512], core.ps[6 + half][0:n, :], gate,
                     None).then_inc(done, 1)

        @block.scalar
        def _(act):
            def first():
                for b in range(2):
                    drain_x(act, range(4), 0, b, xT_act)

            def body(e, before, after):
                for fs in range(FS):
                    for fc in range(4):
                        act.wait_ge(gu_mm, e * 16 + (4 * fs + fc + 1))
                        nc.scalar.activation(sil[fc % 2], core.ps[fc % 2][:, 0:CT], ACT.Silu).then_inc(sil_done, 1)
                    if fs == 0 and before:
                        for b in range(2):
                            if not (isinstance(e, int) and e == 1):
                                act.wait_ge(y_out[b], (e - 1) * 16)
                            drain_y(act, 0, e - 1, b, y_act)
                    if fs == FS - 1 and after:
                        for b in range(2):
                            drain_x(act, range(4), e + 1, b, xT_act)
                drain_yT(act, range(4), e, yT_act)
            first()
            body(0, False, True)
            body(1, True, True)
            with act.Fori(2, NE - 1) as e:
                body(e, True, True)
            body(NE - 1, True, False)
            for b in range(2):
                act.wait_ge(y_out[b], (NE - 1) * 16)
                drain_y(act, 0, NE - 1, b, y_act)

        @block.vector
        def _(dve):
            def first():
                for b in range(2):
                    drain_x(dve, range(4, KD), 0, b, xT_dve)

            def body(e, before, after):
                for fs in range(FS):
                    for fc in range(4):
                        dve.wait_ge(sil_done, e * 16 + (4 * fs + fc + 1))
                        nc.vector.tensor_tensor(hid[fs % 2][:, fc, :], sil[fc % 2], core.ps[fc % 2][:, 256:256 + CT],
                                                ALU.mult).then_inc(hid_done, 1)
                    if fs == 0 and before:
                        for b in range(2):
                            if not (isinstance(e, int) and e == 1):
                                wait_apart(dve, y_out[b], (e - 1) * 16, sem("experts_dve_turns"))
                            drain_y(dve, 1, e - 1, b, y_dve)
                    if fs == FS - 1 and after:
                        for b in range(2):
                            drain_x(dve, range(4, KD), e + 1, b, xT_dve)
                drain_yT(dve, range(4, KD), e, yT_dve)
            first()
            body(0, False, True)
            body(1, True, True)
            with dve.Fori(2, NE - 1) as e:
                body(e, True, True)
            body(NE - 1, True, False)
            for b in range(2):
                dve.wait_ge(y_out[b], (NE - 1) * 16)
                drain_y(dve, 1, NE - 1, b, y_dve)

        @block.tensor
        def _(pe):
            def turn_x(e, b):
                wait_apart(pe, xe_in[b], e * 16 + 16, sem("experts_pe_turns"))
                r = SPLIT[b][0]
                n = CAP[r]
                if b:
                    pe.wait_ge(xT_act, e * 2 + 1)
                    wait_apart(pe, xT_dve, e * 2 + 1, sem("experts_pe_turns"))
                for k in range(KD):
                    mm = nc.tensor.transpose(core.ps[6 + k // 4][:, k % 4 * P:k % 4 * P + n], xe[b][:, k * P:(k + 1) * P],
                                             core.ident[0:n, 0:n])
                mm.then_inc(x_turned, 1)

            def turn_y(e, b):
                r, c0, c1 = SPLIT[b]
                if b:
                    pe.wait_ge(y_act, e * 2 + 1)
                    wait_apart(pe, y_dve, e * 2 + 1, sem("experts_pe_turns"))
                else:
                    pe.wait_ge(yT_act, e + 1)
                    pe.wait_ge(yT_dve, e + 1)
                for dc in range(KD):
                    mm = nc.tensor.transpose(core.ps[6 + dc // 4][0:c1 - c0, dc % 4 * P:(dc % 4 + 1) * P],
                                             yT[:, dc, c0:c1], core.ident)
                mm.then_inc(y_turned, 1)

            def gate_up(e, fs):
                for fc in range(4):
                    n = 4 * fs + fc
                    if fc == 0:
                        for kind in range(2):
                            pe.wait_ge(slab_in[fs % 2][kind], e * 32 + 16 * (fs // 2 + 1))
                    if not (isinstance(e, int) and e == 0 and n < 2):
                        pe.wait_ge(hid_done, e * 16 + (n - 1))
                    for kind in range(2):
                        for k in range(KD):
                            mm = nc.tensor.matmul(core.ps[fc % 2][:, 256 * kind:256 * kind + CT],
                                                  slab[fs % 2][kind][:, k, fc * P:(fc + 1) * P], xT[:, k, :],
                                                  start=(k == 0), stop=(k == KD - 1))
                    mm.then_inc(gu_mm, 1)

            def down(e, fs, fcs):
                for fc in fcs:
                    if fc == 0:
                        pe.wait_ge(slab_in[fs % 2][2], e * 32 + 16 * (fs // 2 + 1))
                    pe.wait_ge(hid_done, e * 16 + (4 * fs + fc + 1))
                    for dc in range(KD):
                        mm = nc.tensor.matmul(y_part(dc), slab[fs % 2][2][:, fc, dc * P:(dc + 1) * P], hid[fs % 2][:, fc, :],
                                              start=(fs == 0 and fc == 0 and dc % 2 == 0), stop=(fs == FS - 1 and fc == 3),
                                              skip_group_check=True)
                if fcs[-1] == 3:
                    mm.then_inc(down_used, 1)

            def body(e, before, after):
                for fs in range(FS):
                    gate_up(e, fs)
                    if fs == 0 and before:
                        turn_y(e - 1, 0)
                    if fs == FS - 1 and after:
                        turn_x(e + 1, 0)
                    down(e, fs, (0, 1))
                    if fs == 0 and before:
                        turn_y(e - 1, 1)
                    if fs == FS - 1 and after:
                        turn_x(e + 1, 1)
                    down(e, fs, (2, 3))

            for b in range(2):
                turn_x(0, b)
            pe.wait_ge(xT_act, 2)
            pe.wait_ge(xT_dve, 2)
            body(0, False, True)
            with pe.Fori(1, NE - 1) as e:
                pe.wait_ge(xT_act, e * 2 + 2)
                pe.wait_ge(xT_dve, e * 2 + 2)
                body(e, True, True)
            pe.wait_ge(xT_act, NE * 2)
            pe.wait_ge(xT_dve, NE * 2)
            body(NE - 1, True, False)
            for b in range(2):
                turn_y(NE - 1, b)


def final(core, A):
    nc, io, sem = core.nc, core.io, core.sem
    x = [A.at(D * j, D) for j in range(4)]
    y = [A.at(D * (4 + j), D) for j in range(4)]
    weight, junk = A.at(8 * D, D), A.at(9 * D, D)
    ss, rms, rstd = (core.small(f"final_{n}", [P, 4]) for n in ("ss", "rms", "rstd"))
    x_in, stored = ([sem(f"{n}{j}") for j in range(4)] for n in ("final_in", "final_out"))
    row_mm, row_done, act_order, root, y_done, x_free = (
        sem(n) for n in ("final_row_mm", "final_row", "final_act_order", "final_root", "final_y", "final_free"))

    def tiles(eng, body):
        for r, (lo, hi) in enumerate(TILES):
            if hi - lo == 4:
                for j in range(4):
                    body(lo + j, j, r)
            else:
                with eng.Fori(lo // 4, hi // 4) as turn:
                    for j in range(4):
                        body(turn * 4 + j, j, r)

    with nc.Block() as block:
        @block.sync
        def _(sp):
            def body(g, j, r):
                sp.wait_ge(x_free, g + 1)
                sp.dma_start(x[j], core.residual[bass.ds(g * P, P), :]).then_inc(x_in[j], 16)
            tiles(sp, body)

        @block.gpsimd
        def _(pool):
            def body(g, j, r):
                pool.wait_ge(y_done, g + 1)
                out = (io["y_prompt"], io["y_sample"])[r][0]
                pool.dma_start(out[bass.ds((g - TILES[r][0]) * P, P), :], y[j]).then_inc(stored[j], 16)
            tiles(pool, body)
            for j in range(4):
                pool.wait_ge(stored[j], NT // 4 * 16)

        @block.scalar
        def _(act):
            def body(g, j, r):
                act.wait_ge(x_in[j], (g - j) * 4 + 16)
                nc.scalar.activation(junk, x[j], ACT.Square, accum_out=ss[:, j:j + 1]).then_inc(act_order, 1)
                act.wait_ge(act_order, g + 1)
                nc.scalar.activation(rms[:, j:j + 1], ss[:, j:j + 1], ACT.Sqrt, bias=core.eps[:, 0:1],
                                     scale=1.0 / D).then_inc(root, 1)
            tiles(act, body)

        @block.vector
        def _(dve):
            dve.sem_inc(x_free, 4)
            for half in range(2):
                dve.wait_ge(row_mm, half + 1)
                nc.vector.tensor_copy(weight[:, 512 * half:512 * half + 512], core.ps[half]).then_inc(row_done, 1)
            dve.wait_ge(row_done, 2)

            def body(g, j, r):
                dve.wait_ge(root, g + 1)
                nc.vector.reciprocal(rstd[:, j:j + 1], rms[:, j:j + 1]).then_inc(sem("final_rstd"), 1)
                if not (isinstance(g, int) and g < 4):
                    dve.wait_ge(stored[j], (g - j) * 4)
                dve.wait_ge(sem("final_rstd"), g + 1)
                nc.vector.scalar_tensor_tensor(out=y[j], in0=x[j], scalar=rstd[:, j:j + 1], in1=weight, op0=ALU.mult,
                                               op1=ALU.mult).then_inc(y_done, 1)
                dve.wait_ge(y_done, g + 1)
                dve.sem_inc(x_free, 1)
            tiles(dve, body)

        @block.tensor
        def _(pe):
            for half in range(2):
                for k in range(4 * half, 4 * half + 4):
                    mm = row_of(nc, core.ps[half], core.col("final", k), k, 0, core.ident)
                mm.then_inc(row_mm, 1)


STAGES = [modulation, projections, convolution, states, ssd, attend, output, choice, experts, final]


def encoder_layer(nc, io, stages=None):
    with ExitStack() as ctx:
        core = Core(nc, ctx, io)
        arena = Arena(ctx.enter_context(nc.sbuf_tensor("arena", [P, ARENA], F32)), ARENA)
        for stage in (stages or STAGES):
            if stage is output:
                core.release()
            with ExitStack() as core.stage:
                stage(core, arena)
        core.release()


_BIG = ["x_prompt", "x_sample", "w_ada", "w_in", "w_uq", "w_ukv", "w_out", "w_router", "w_gate", "w_up", "w_down"]
_OUTS = [("y_prompt", (1, 512, 1024)), ("y_sample", (1, 1024, 1024))]


def packed(inputs):
    import numpy as np

    names = [("c_prompt",), ("c_sample",), ("norm1_w",), ("norm2_w",), ("final_norm_w",), ("q_norm_w",),
             ("kv_norm_w",), ("attn_norm_w",), ("ssd_norm_w",), ("conv_b",), ("conv_w",), ("b_ada",)]
    rows = np.concatenate([np.asarray(inputs[n[0]]).reshape(-1, P) for n in names])
    k, m = np.arange(P)[:, None], np.arange(P)[None, :]
    masks = np.stack([k == m, k <= m, k > m, k >= m, k < m, k < P + m], axis=1).astype(np.float32)
    vec = np.concatenate([np.asarray(inputs[n]).reshape(-1) for n in ("dt_bias", "a_log", "d_skip")])
    inv = (1.0 / (10000.0 ** (np.arange(0, DR, 2, dtype=np.float32) / DR))).astype(np.float32)
    ang = np.arange(1024, dtype=np.float32)[:, None] * inv[None, :]
    rope = np.stack([np.cos(ang), np.sin(ang)], axis=1).astype(np.float32)
    return {
        "p_cols": np.ascontiguousarray(rows.T),
        "p_masks": np.ascontiguousarray(masks),
        "p_rows": np.ascontiguousarray(np.broadcast_to(vec, (P, NROW))),
        "p_rope": np.ascontiguousarray(rope.reshape(8, P, 2, 16).transpose(1, 0, 2, 3)),
    }


def kernel(**inputs):
    import numpy as np
    import concourse.bacc as bacc
    from concourse.bass_utils import run_bass_kernel_spmd

    nc = bacc.Bacc("TRN2", target_bir_lowering=False, num_devices=1)
    arrays = {n: np.ascontiguousarray(inputs[n]) for n in _BIG}
    arrays.update(packed(inputs))
    io = {n: nc.dram_tensor(n, a.shape, mybir.dt.from_np(a.dtype), kind="ExternalInput").ap() for n, a in arrays.items()}
    for name, shape in _OUTS:
        io[name] = nc.dram_tensor(name, shape, F32, kind="ExternalOutput").ap()
    encoder_layer(nc, io)
    r = run_bass_kernel_spmd(nc, [arrays], core_ids=[0])
    return tuple(r.results[0][name] for name, _ in _OUTS)
```

```python
from contextlib import ExitStack

import concourse.bass as bass
from concourse import mybir

ALU = mybir.AluOpType
ACT = mybir.ActivationFunctionType
AX_X = mybir.AxisListType.X
F32 = mybir.dt.float32
U32 = mybir.dt.uint32

P = 128
D = 1024
KD = D // P
T_OF = (512, 1024)
NT = sum(T_OF) // P
TILES = ((0, 4), (4, 12))
NH, DN, DR, DV = 8, 64, 32, 64
DQK = DN + DR
QL, KVL = 256, 128
NS, HP, DS = 8, 64, 64
DSSD = NS * HP
CONV = DSSD + 2 * 2 * DS
KC = CONV // P
TAPS = 5
NAT = QL + KVL + DR
Z0, X0, DT0 = NAT, NAT + DSSD, NAT + DSSD + CONV
DIN = DT0 + 2 * NS
NE, FE = 16, 2048
CAP = (64, 128)
EPS = 1e-6
SCALE = float(DQK) ** -0.5
SPANS = ((0, 2, 0), (2, 4, 0), (4, 10, 1), (10, 12, 1))

COLS = {}
_at = 0
for _name, _n in (("c", 2 * KD), ("norm1", KD), ("norm2", KD), ("final", KD), ("q_norm", 2), ("kv_norm", 1),
                  ("attn_norm", 4), ("ssd_norm", 4), ("conv_b", KC), ("conv_w", TAPS * KC), ("b_ada", 6 * KD)):
    COLS[_name] = (_at, _at + _n)
    _at += _n
NCOL = _at
ROW_DTB, ROW_ALOG, ROW_D, NROW = 0, 16, 32, 40
M_ID, M_LE, M_GT, M_GE, M_LT, M_ONE = range(6)
D_CSF, D_CSB, D_OUTF, D_OUTB, D_TOT = range(5)
PADT = 4
XW = NT * P + 2 * PADT


def tile_loop(eng, body):
    for lo, hi, request in SPANS:
        if hi - lo == 2:
            body(lo, 0, request)
            body(lo + 1, 1, request)
        else:
            with eng.Fori(lo // 2, hi // 2) as turn:
                body(turn * 2, 0, request)
                body(turn * 2 + 1, 1, request)


def tile_loop_ahead(eng, front, back):
    front(0, 0, 0)
    for lo, hi, request in SPANS:
        def pair(g, after):
            front(g + 1, 1, request)
            back(g, 0, request)
            if after is not None:
                front(g + 2, 0, after)
            back(g + 1, 1, request)
        if hi - lo == 2:
            pair(lo, None if hi == NT else 1 if hi == TILES[1][0] else request)
        else:
            with eng.Fori(lo // 2, hi // 2) as turn:
                pair(turn * 2, request)


def tile_pipeline(eng, phases):
    least, most = min(ahead for ahead, _ in phases), max(ahead for ahead, _ in phases)

    def alone(t):
        for ahead, step in phases:
            if 0 <= t + ahead < NT:
                step(t + ahead, (t + ahead) % 2, int(t + ahead >= TILES[1][0]))
    lo, hi = (TILES[1][0] - least + 1) // 2, (NT - most) // 2
    for t in range(-most, 2 * lo):
        alone(t)
    with eng.Fori(lo, hi) as i:
        for j in range(2):
            for ahead, step in phases:
                step(i * 2 + (j + ahead), (j + ahead) % 2, 1)
    for t in range(2 * hi, NT - least):
        alone(t)


def request_pipeline(eng, r, phases):
    first, n = TILES[r][0], TILES[r][1] - TILES[r][0]
    least, most = min(ahead for ahead, _ in phases), max(ahead for ahead, _ in phases)

    def alone(t):
        for ahead, step in phases:
            if 0 <= t + ahead < n:
                step(first + t + ahead, t + ahead, (t + ahead) % 2)
    lo = (1 - least) // 2
    hi = max(lo, (n - most) // 2)
    for t in range(-most, 2 * lo):
        alone(t)
    if hi > lo:
        with eng.Fori(lo, hi) as i:
            for j in range(2):
                for ahead, step in phases:
                    step(i * 2 + (first + j + ahead), i * 2 + (j + ahead), (j + ahead) % 2)
    for t in range(2 * hi, n - least):
        alone(t)


def wait_apart(eng, sem, value, turns):
    eng.wait_ge(sem, value)
    eng.sem_inc(turns, 1)


class Order:

    def __init__(self, eng, sem, base=0):
        self.eng, self.sem, self.base, self.n = eng, sem, base, 0

    def link(self, ins):
        self.n += 1
        ins.then_inc(self.sem, 1)
        self.eng.wait_ge(self.sem, self.base + self.n)


class Core:

    def __init__(self, nc, ctx, io):
        self.nc, self.ctx, self.io = nc, ctx, io
        self.banks = ctx.enter_context(nc.psum_tensor("banks", [P, 8 * 512], F32))
        self.ps = [self.banks[:, 512 * i:512 * i + 512] for i in range(8)]
        self.masks = self.sbuf("masks", [P, 6, P])
        self.cols = self.sbuf("cols", [P, NCOL])
        self.rows = self.sbuf("rows", [P, NROW])
        self.rope = self.sbuf("rope", [P, 8, 2, 16])
        self.mod = self.sbuf("mod", [P, 6 * KD, 2])
        self.scale1 = self.sbuf("scale1", [P, KD, 2])
        self.scale2 = self.sbuf("scale2", [P, KD, 2])
        self.eps = self.sbuf("eps", [P, 2])
        self.tot = self.sbuf("chunk_decay", [P, NT, 2, 4])
        self.chosen = self.sbuf("chosen", [P, 48], U32)
        self.gates = self.sbuf("gates", [P, 48])
        self.residual, self.normed = self.dram("residual", [NT * P, D]), self.dram("normed", [NT * P, D])
        self.sems = {}
        self.ident = self.masks[:, M_ID, :]

    def sbuf(self, name, shape, dtype=F32):
        return self.ctx.enter_context(self.nc.sbuf_tensor(name, shape, dtype))

    def small(self, name, shape, dtype=F32):
        return self.stage.enter_context(self.nc.sbuf_tensor(name, shape, dtype))

    def sem(self, name):
        if name not in self.sems:
            self.sems[name] = self.nc.alloc_semaphore(name)
        return self.sems[name]

    def release(self):
        self.nc.clear_and_free_semaphores(list(self.sems.values()))
        self.nc.all_engine_barrier()
        self.sems = {}

    def col(self, name, k=0):
        a, _ = COLS[name]
        return self.cols[:, a + k:a + k + 1]

    def dram(self, name, shape):
        return self.nc.dram_tensor(name, shape, F32, kind="Internal").ap()


class Arena:

    def __init__(self, tensor, size):
        self.t, self.size = tensor, size

    def at(self, start, *dims):
        n = 1
        for d in dims:
            n *= d
        assert start + n <= self.size, (start, n, self.size)
        v = self.t[:, start:start + n]
        names = ["a", "b", "c", "d"][:len(dims)]
        if len(dims) == 1:
            return v
        return v.rearrange(f"p ({' '.join(names)}) -> p {' '.join(names)}", **dict(zip(names, dims)))


ARENA = 49920
A_WIN = 0
A_X, A_XN, A_HT, A_JUNK = 13696, 15744, 17792, 19840
A_RING = 25984
A_NAT = 25984
A_DT = A_NAT + NAT * NT
A_Z = A_DT + 2 * NS * NT
A_XBC = A_Z + DSSD * NT
A_MODROW = A_RING + 4 * 4096
SLABS = 4


def modulation(core, A):
    nc, io, sem = core.nc, core.io, core.sem
    ring = [A.at(A_RING + 4096 * s, KD, 512) for s in range(SLABS)]
    slab_in = [sem(f"ada_slab_in{s}") for s in range(SLABS)]
    slab_used, silu_c, consts_in = sem("ada_slab_used"), sem("silu_c"), sem("consts_in")
    dve_order = sem("mod_dve_order")
    sc = core.small("silu_c_cols", [P, KD, 2])
    rows = A.at(A_MODROW, 6 * D)[0:2]
    rows_done, cols_mm = sem("mod_rows"), sem("mod_cols_mm")
    w = io["w_ada"][0].rearrange("(k p) n -> p k n", p=P)
    c_cols = core.cols[:, 0:2 * KD].rearrange("p (r k) -> p k r", r=2)

    with nc.Block() as block:
        @block.sync
        def _(sp):
            for name, t in (("p_masks", core.masks), ("p_cols", core.cols), ("p_rows", core.rows), ("p_rope", core.rope)):
                sp.dma_start(t[:], io[name]).then_inc(consts_in, 16)
            for s in range(SLABS):
                sp.dma_start(ring[s], w[:, :, s * 512:s * 512 + 512]).then_inc(slab_in[s], 16)
            with sp.Fori(1, 12 // SLABS) as turn:
                for s in range(SLABS):
                    sp.wait_ge(slab_used, turn * SLABS + (s + 1 - SLABS))
                    sp.dma_start(ring[s], w[:, :, bass.ds((turn * SLABS + s) * 512, 512)]).then_inc(slab_in[s], 16)
            w_in = A.at(A_WIN, KD, DIN)
            src = io["w_in"][0].rearrange("(k p) n -> p k n", p=P)
            for h in range(2):
                sp.dma_start(w_in[:, 4 * h:4 * h + 4, :], src[:, 4 * h:4 * h + 4, :]).then_inc(sem("w_in_in"), 16)

        @block.scalar
        def _(act):
            act.wait_ge(consts_in, 64)
            nc.scalar.activation(sc[:], c_cols, ACT.Silu).then_inc(silu_c, 1)

        @block.tensor
        def _(pe):
            pe.wait_ge(silu_c, 1)
            pe.sem_inc(sem("mod_pe_turns"), 1)
            with pe.Fori(0, 12 // SLABS) as turn:
                for s in range(SLABS):
                    pe.wait_ge(slab_in[s], turn * 16 + 16)
                    pe.wait_ge(rows_done, turn * SLABS + (s + 1))
                    for k in range(KD):
                        mm = nc.tensor.matmul(core.ps[s][0:2, :], sc[:, k, :], ring[s][:, k, :],
                                              start=(k == 0), stop=(k == KD - 1))
                    mm.then_inc(slab_used, 1)
            pe.wait_ge(rows_done, SLABS + 12)
            for j in range(6 * KD):
                mm = nc.tensor.transpose(core.ps[4][:, 2 * j:2 * j + 2], rows[:, j * P:(j + 1) * P], core.ident[0:2, 0:2])
            mm.then_inc(cols_mm, 1)

        @block.vector
        def _(dve):
            order = Order(dve, dve_order)
            dve.sem_inc(rows_done, SLABS)
            nc.vector.memset(core.eps[:, 0:1], EPS)
            nc.vector.memset(core.eps[:, 1:2], 1.0)
            with dve.Fori(0, 12 // SLABS) as turn:
                for s in range(SLABS):
                    dve.wait_ge(slab_used, turn * SLABS + (s + 1))
                    nc.vector.tensor_copy(rows[:, bass.ds(turn * (512 * SLABS) + 512 * s, 512)],
                                          core.ps[s][0:2, :]).then_inc(rows_done, 1)
            dve.wait_ge(consts_in, 64)
            dve.wait_ge(cols_mm, 1)
            b0, b1 = COLS["b_ada"]
            bias = core.cols[:, b0:b1].unsqueeze(2).broadcast_to([P, 6 * KD, 2])
            order.link(nc.vector.tensor_tensor(core.mod[:], core.ps[4][:, 0:12 * KD].rearrange("p (j r) -> p j r", r=2),
                                               bias, ALU.add))
            for name, out, at in (("norm1", core.scale1, KD), ("norm2", core.scale2, 4 * KD)):
                n0, n1 = COLS[name]
                gain = core.cols[:, n0:n1].unsqueeze(2).broadcast_to([P, KD, 2])
                order.link(nc.vector.tensor_scalar(out[:], core.mod[:, at:at + KD, :], 1.0, None, ALU.add))
                order.link(nc.vector.tensor_tensor(out[:], out[:], gain, ALU.mult))


def load_tile(sp, dst, x_of, g, request, sem):
    return sp.dma_start(dst, x_of[request][0][bass.ds((g - TILES[request][0]) * P, P), :]).then_inc(sem, 16)


def projections(core, A):
    nc, io, sem = core.nc, core.io, core.sem
    w_in = A.at(A_WIN, KD, DIN)
    x = [A.at(A_X + D * j, D) for j in range(2)]
    xn = [A.at(A_XN + D * j, D) for j in range(2)]
    hT = [A.at(A_HT + D * j, KD, P) for j in range(2)]
    junk = A.at(A_JUNK, D)
    nat = A.at(A_NAT, NT * NAT)
    dt = A.at(A_DT, NT * 2 * NS)
    z = A.at(A_Z, NT * DSSD)
    xbc = A.at(A_XBC, KC, XW)
    ss, rms, rstd = (core.small(f"proj_{n}", [P, 2]) for n in ("ss", "rms", "rstd"))
    x_in = [sem(f"x_in{j}") for j in range(2)]
    sumsq, root, x_free, xn_ready = sem("x_sumsq"), sem("x_root"), sem("x_free"), sem("xn_ready")
    turned, hT_act, hT_dve = sem("xn_turned"), sem("hT_act"), sem("hT_dve")
    nat_done, z_done, xbc_done = sem("nat_done"), sem("z_done"), sem("xbc_done")
    banks_act, banks_dve = sem("proj_banks_act"), sem("proj_banks_dve")
    dve_order = sem("proj_dve_order")
    x_of = (io["x_prompt"], io["x_sample"])
    b_nat, b_z, b_x = core.ps[2], core.ps[3], core.ps[4:6]

    with nc.Block() as block:
        @block.sync
        def _(sp):
            def body(g, j, r):
                sp.wait_ge(x_free, g + 1)
                load_tile(sp, x[j], x_of, g, r, x_in[j])
            tile_loop(sp, body)

        @block.scalar
        def _(act):
            act.sem_inc(banks_act, 1)

            def stats(g, j, r):
                act.wait_ge(x_in[j], (g - j) * 8 + 16)
                nc.scalar.activation(junk, x[j], ACT.Square, accum_out=ss[:, j:j + 1]).then_inc(sumsq, 1)
                act.wait_ge(sumsq, g + 1)
                nc.scalar.activation(rms[:, j:j + 1], ss[:, j:j + 1], ACT.Sqrt, bias=core.eps[:, 0:1],
                                     scale=1.0 / D).then_inc(root, 1)

            def shift(g, j, r):
                act.wait_ge(turned, g + 1)
                for k in range(4):
                    ins = nc.scalar.activation(hT[j][:, k, :], core.ps[0][:, k * P:(k + 1) * P], ACT.Identity,
                                               bias=core.mod[:, k, r:r + 1], scale=core.scale1[:, k, r:r + 1])
                ins.then_inc(hT_act, 1)

            def back(g, j, r):
                act.wait_ge(nat_done, g + 1)
                nc.scalar.activation(nat[:, bass.ds(g * NAT, NAT)], b_nat[:, 0:NAT], ACT.Copy)
                nc.scalar.activation(dt[:, bass.ds(g * 16, 16)], b_nat[:, NAT:NAT + 16], ACT.Copy)
                act.wait_ge(z_done, g + 1)
                nc.scalar.activation(z[:, bass.ds(g * DSSD, DSSD)], b_z[:, :], ACT.Copy).then_inc(banks_act, 1)
            tile_pipeline(act, [(1, shift), (2, stats), (0, back)])

        @block.vector
        def _(dve):
            dve.sem_inc(x_free, 2)
            dve.sem_inc(banks_dve, 1)
            for at in (0, 4 * P + 2, 4 * P + 4, XW - 2):
                nc.vector.memset(xbc[:, :, at:at + 2], 0.0)

            def scale(g, j, r):
                dve.wait_ge(root, g + 1)
                nc.vector.reciprocal(rstd[:, j:j + 1], rms[:, j:j + 1]).then_inc(dve_order, 1)
                dve.wait_ge(dve_order, g + 1)
                nc.vector.tensor_scalar(xn[j], x[j], rstd[:, j:j + 1], None, ALU.mult).then_inc(xn_ready, 1)
                dve.wait_ge(xn_ready, g + 1)
                dve.sem_inc(x_free, 1)

            def shift(g, j, r):
                dve.wait_ge(turned, g + 1)
                for k in range(4, KD):
                    ins = nc.vector.tensor_scalar(hT[j][:, k, :], core.ps[1][:, (k - 4) * P:(k - 3) * P],
                                                  core.scale1[:, k, r:r + 1], core.mod[:, k, r:r + 1],
                                                  ALU.mult, ALU.add)
                ins.then_inc(hT_dve, 1)

            def back(g, j, r):
                dve.wait_ge(xbc_done, g + 1)
                for c in range(2):
                    ins = nc.vector.tensor_copy(xbc[:, 3 * c:3 * c + 3, bass.ds(g * P + (2 + 4 * r), P)],
                                                b_x[c][:, 0:3 * P].rearrange("p (c t) -> p c t", c=3))
                ins.then_inc(banks_dve, 1)
            tile_pipeline(dve, [(1, shift), (2, scale), (0, back)])

        @block.tensor
        def _(pe):
            pe.wait_ge(sem("w_in_in"), 32)

            def front(g, j, r):
                pe.wait_ge(xn_ready, g + 1)
                for k in range(KD):
                    mm = nc.tensor.transpose(core.ps[k // 4][:, k % 4 * P:(k % 4 + 1) * P],
                                             xn[j][:, k * P:(k + 1) * P], core.ident)
                mm.then_inc(turned, 1)

            def back(g, j, r):
                pe.wait_ge(hT_act, g + 1)
                pe.wait_ge(hT_dve, g + 1)
                pe.wait_ge(banks_act, g + 1)
                for lo, hi, at in ((0, NAT, 0), (DT0, DIN, NAT)):
                    for k in range(KD):
                        mm = nc.tensor.matmul(b_nat[:, at:at + hi - lo], hT[j][:, k, :], w_in[:, k, lo:hi],
                                              start=(k == 0), stop=(k == KD - 1))
                mm.then_inc(nat_done, 1)
                for k in range(KD):
                    mm = nc.tensor.matmul(b_z[:, :], hT[j][:, k, :], w_in[:, k, Z0:X0],
                                          start=(k == 0), stop=(k == KD - 1))
                mm.then_inc(z_done, 1)
                pe.wait_ge(banks_dve, g + 1)
                for c in range(KC):
                    for k in range(KD):
                        mm = nc.tensor.matmul(b_x[c // 3][:, c % 3 * P:(c % 3 + 1) * P],
                                              w_in[:, k, X0 + c * P:X0 + (c + 1) * P], hT[j][:, k, :],
                                              start=(k == 0), stop=(k == KD - 1))
                mm.then_inc(xbc_done, 1)
            tile_pipeline(pe, [(1, front), (0, back)])


A_XC = 0
A_STB = 9216
A_STF = 13696
A_CT = A_STF + 256 * (NT + 2)
A_DEC = A_CT + NT * P
A_DTS = A_STB + 256 * (NT + 2)
A_DTA, A_W = A_DTS + 16 * NT, A_DTS + 32 * NT
A_XNAT = A_XBC
A_CB = A_XBC + DSSD * NT
A_TAIL = A_XBC + KC * XW
A_MIX = 13696
G16 = 16 * NT


def convolution(core, A):
    nc, sem = core.nc, core.sem
    xbc, xc = A.at(A_XBC, KC, XW), A.at(A_XC, KC, NT * P)
    z = A.at(A_Z, NT * DSSD)
    dt_raw, dt, dta, w = (A.at(a, NT, 16) for a in (A_DT, A_DTS, A_DTA, A_W))
    dec = A.at(A_DEC, 5, NT, 16)
    flat = [core.small(f"soft{i}", [P, NT, 16]) for i in range(4)]
    a_pos = core.small("a_pos", [P, 16])
    tot = core.tot
    tap0, tap_order = sem("conv_tap0"), sem("conv_order")
    soft_v, soft_e, soft_ln, steps, decays = (sem(n) for n in ("soft_v", "soft_e", "soft_ln", "steps", "decays"))
    dec_mm = sem("dec_mm")
    cw = COLS["conv_w"][0]
    seqs = [(2 + PADT * r + TILES[r][0] * P, T_OF[r], TILES[r][0] * P) for r in range(2)]

    with nc.Block() as block:
        @block.scalar
        def _(act):
            act.preload_act_table_set("natural_log_exp_and_others")
            act.wait_ge(soft_v, 1)
            nc.scalar.activation(flat[1][:], flat[1][:], ACT.Exp, scale=-1.0).then_inc(soft_e, 1)
            nc.scalar.activation(a_pos[:], core.rows[:, ROW_ALOG:ROW_ALOG + 16], ACT.Exp).then_inc(soft_e, 1)
            act.wait_ge(soft_v, 2)
            nc.scalar.activation(flat[3][:], flat[2][:], ACT.Ln).then_inc(soft_ln, 1)
            with act.Fori(0, KC) as c:
                for at, n, to in seqs:
                    nc.scalar.activation(xc[:, bass.ds(c, 1), to:to + n], xbc[:, bass.ds(c, 1), at - 2:at - 2 + n],
                                         ACT.Copy, scale=core.cols[:, bass.ds(c + cw, 1)]).then_inc(tap0, 1)
            act.wait_ge(dec_mm, 1)
            for kind in range(5):
                ins = nc.scalar.activation(dec[:, kind], core.ps[kind // 2][:, kind % 2 * G16:(kind % 2 + 1) * G16]
                                           .rearrange("p (g h) -> p g h", h=16), ACT.Exp)
            ins.then_inc(decays, 1)
            for q in range(4):
                n = NT * DSSD // 4
                nc.scalar.activation(z[:, q * n:(q + 1) * n], z[:, q * n:(q + 1) * n], ACT.Silu)

        @block.vector
        def _(dve):
            order = Order(dve, sem("soft_order"))
            v, m, one_e, ln = flat
            bias = core.rows[:, ROW_DTB:ROW_DTB + 16].unsqueeze(1).broadcast_to([P, NT, 16])
            order.link(nc.vector.tensor_tensor(v[:], dt_raw, bias, ALU.add))
            nc.vector.scalar_tensor_tensor(out=m[:], in0=v[:], scalar=-1.0, in1=v[:], op0=ALU.mult,
                                           op1=ALU.max).then_inc(soft_v, 1)
            dve.wait_ge(soft_e, 2)
            order.link(nc.vector.tensor_scalar(one_e[:], m[:], 1.0, None, ALU.add))
            dve.sem_inc(soft_v, 1)
            order.link(nc.vector.tensor_scalar(dta, one_e[:], -1.0, None, ALU.add))
            order.link(nc.vector.tensor_scalar(w, dta, 0.0, None, ALU.is_equal))
            order.link(nc.vector.tensor_tensor(dta, dta, w, ALU.add))
            order.link(nc.vector.reciprocal(dta, dta))
            order.link(nc.vector.tensor_tensor(dta, dta, m[:], ALU.mult))
            dve.wait_ge(soft_ln, 1)
            order.link(nc.vector.tensor_tensor(w, w, ln[:], ALU.add))
            order.link(nc.vector.tensor_tensor(w, w, dta, ALU.mult))
            order.link(nc.vector.scalar_tensor_tensor(out=dt, in0=v[:], scalar=0.0, in1=w, op0=ALU.max, op1=ALU.add))
            a = a_pos[:].unsqueeze(1).broadcast_to([P, NT, 16])
            nc.vector.scalar_tensor_tensor(out=dta, in0=dt, scalar=-1.0, in1=a, op0=ALU.mult,
                                           op1=ALU.mult).then_inc(steps, 1)
            with dve.Fori(0, KC) as c:
                for tap in range(1, TAPS):
                    for r, (at, n, to) in enumerate(seqs):
                        if tap == 1:
                            dve.wait_ge(tap0, c * 2 + (r + 1))
                        else:
                            dve.wait_ge(tap_order, c * 8 + (2 * (tap - 2) + r + 1))
                        out = xc[:, bass.ds(c, 1), to:to + n]
                        nc.vector.scalar_tensor_tensor(
                            out=out, in0=xbc[:, bass.ds(c, 1), at - 2 + tap:at - 2 + tap + n],
                            scalar=core.cols[:, bass.ds(c + (cw + tap * KC), 1)], in1=out,
                            op0=ALU.mult, op1=ALU.add).then_inc(tap_order, 1)
            dve.wait_ge(decays, 1)
            nc.vector.tensor_tensor(w[:, :, 0:8], dec[:, D_OUTF, :, 0:8], dt[:, :, 0:8], ALU.mult)
            nc.vector.tensor_tensor(w[:, :, 8:16], dec[:, D_OUTB, :, 8:16], dt[:, :, 8:16], ALU.mult)
            for half in range(2):
                rows = slice(64 * half, 64 * half + 64)
                src = dec[rows, D_TOT].rearrange("p g (d h) -> p g d h", d=2)[:, :, :, 4 * half:4 * half + 4]
                nc.vector.tensor_copy(tot[rows], src)

        @block.tensor
        def _(pe):
            pe.wait_ge(steps, 1)
            for kind, m in ((D_CSF, M_LE), (D_CSB, M_GE), (D_OUTF, M_GT), (D_OUTB, M_LT), (D_TOT, M_ONE)):
                mm = nc.tensor.matmul(core.ps[kind // 2][:, kind % 2 * G16:(kind % 2 + 1) * G16],
                                      core.masks[:, m, :], dta.rearrange("p g h -> p (g h)"), start=True, stop=True)
            mm.then_inc(dec_mm, 1)


def slot_in(g, r, back):
    return (g + (r + back)) * 256


def slot_out(g, r, back):
    return (g + (r + 1 - back)) * 256


def states(core, A):
    nc, sem = core.nc, core.sem
    xc = A.at(A_XC, KC, NT * P)
    ct = A.at(A_CT, NT * P)
    st = [A.at(A_STF, 256 * (NT + 2)), A.at(A_STB, 256 * (NT + 2))]
    w = A.at(A_W, G16)
    xnat, cb = A.at(A_XNAT, NT * DSSD), A.at(A_CB, NT * 256)
    xct = [A.at(A_TAIL + KC * P * j, KC, P) for j in range(2)]
    xw = A.at(A_TAIL + 2 * KC * P, 2, DSSD)
    bn = [core.small(f"b_nat{j}", [P, P]) for j in range(2)]
    btz = [core.small(f"b_groups{j}", [P, 2, P]) for j in range(2)]
    silu_done, btz_done, turned, cb_done = sem("silu_done"), sem("b_groups_done"), sem("x_turned"), sem("cb_done")
    xnat_done, xw_done, state_mm, state_out = sem("xnat_done"), sem("xw_done"), sem("state_mm"), sem("state_out")
    bn_done = sem("b_nat_done")

    with nc.Block() as block:
        @block.scalar
        def _(act):
            def front(g, j, r):
                for c in range(KC):
                    b = COLS["conv_b"][0] + c
                    ins = nc.scalar.activation(xct[j][:, c, :], xc[:, c, bass.ds(g * P, P)], ACT.Silu,
                                               bias=core.cols[:, b:b + 1])
                ins.then_inc(silu_done, 1)

            def back(g, j, r):
                act.wait_ge(turned, g + 1)
                nc.scalar.activation(xnat[:, bass.ds(g * DSSD, DSSD)], core.ps[j][:, :], ACT.Copy).then_inc(xnat_done, 1)
                act.wait_ge(cb_done, g + 1)
                act.wait_ge(bn_done, g + 1)
            tile_loop_ahead(act, front, back)

        @block.vector
        def _(dve):
            for t in btz:
                nc.vector.memset(t[0:64, 1, :], 0.0)
                nc.vector.memset(t[64:128, 0, :], 0.0)
            for r in range(2):
                lo, hi = TILES[r]
                nc.vector.memset(st[0][:, slot_in(lo, r, 0):slot_in(lo, r, 0) + 256], 0.0)
                nc.vector.memset(st[1][:, slot_in(hi - 1, r, 1):slot_in(hi - 1, r, 1) + 256], 0.0)

            def front(g, j, r):
                dve.wait_ge(silu_done, g + 1)
                nc.vector.tensor_copy(btz[j][0:64, 0, :], xct[j][0:64, 4, :])
                nc.vector.tensor_copy(btz[j][64:128, 1, :], xct[j][64:128, 4, :])
                nc.vector.tensor_copy(ct[:, bass.ds(g * P, P)], xct[j][:, 5, :]).then_inc(btz_done, 1)

            def back(g, j, r):
                dve.wait_ge(cb_done, g + 1)
                nc.vector.tensor_copy(cb[:, bass.ds(g * 256, 256)], core.ps[2 + j][:, P:3 * P])
                nc.vector.tensor_copy(bn[j][:], core.ps[2 + j][:, 0:P]).then_inc(bn_done, 1)
                dve.wait_ge(xnat_done, g + 1)
                for d in range(2):
                    nc.vector.tensor_tensor(
                        xw[:, d].rearrange("p (h e) -> p h e", h=NS),
                        xnat[:, bass.ds(g * DSSD, DSSD)].rearrange("p (h e) -> p h e", h=NS),
                        w[:, bass.ds(g * 16 + 8 * d, 8)].unsqueeze(2).broadcast_to([P, NS, HP]),
                        ALU.mult).then_inc(xw_done, 1)
                dve.wait_ge(state_mm, g + 1)
                for d in range(2):
                    ins = nc.vector.tensor_copy(st[d][:, bass.ds(slot_out(g, r, d), 256)], core.ps[4 + d][:, 0:256])
                ins.then_inc(state_out, 1)
            tile_loop_ahead(dve, front, back)

            dve.wait_ge(state_out, NT)
            scan(dve, nc, core, st, A.at(A_XC, 2, 256), sem("scan_order"), sem("scan_turns"))

        @block.tensor
        def _(pe):
            def front(g, j, r):
                pe.wait_ge(silu_done, g + 1)
                for c in range(4):
                    mm = nc.tensor.transpose(core.ps[j][:, c * P:(c + 1) * P], xct[j][:, c, :], core.ident)
                mm.then_inc(turned, 1)
                nc.tensor.transpose(core.ps[2 + j][:, 0:P], xct[j][:, 4, :], core.ident)
                pe.wait_ge(btz_done, g + 1)
                for grp in range(2):
                    mm = nc.tensor.matmul(core.ps[2 + j][:, (1 + grp) * P:(2 + grp) * P], btz[j][:, grp, :],
                                          xct[j][:, 5, :], start=True, stop=True)
                mm.then_inc(cb_done, 1)

            def back(g, j, r):
                pe.wait_ge(xw_done, g * 2 + 2)
                for d in range(2):
                    for grp in range(2):
                        mm = nc.tensor.matmul(core.ps[4 + d][64 * grp:64 * grp + 64, 0:256],
                                              bn[j][:, 64 * grp:64 * grp + 64], xw[:, d, 256 * grp:256 * grp + 256],
                                              start=True, stop=True)
                mm.then_inc(state_mm, 1)
            tile_loop_ahead(pe, front, back)


def scan(dve, nc, core, st, tmp, order, turns):
    dve.sem_inc(order, 2)
    tot = core.tot[:].rearrange("p g d h -> p (g d h)")
    done = 0
    for r, (lo, hi) in enumerate(TILES):
        with dve.Fori(0, hi - lo) as i:
            tiles = (i + lo, (hi - 1) - i)
            for d, g in enumerate(tiles):
                wait_apart(dve, order, i * 4 + (done + 1 + d), turns)
                decay = tot[:, bass.ds(g * 8 + 4 * d, 4)].unsqueeze(2).broadcast_to([P, 4, HP])
                nc.vector.tensor_tensor(tmp[:, d].rearrange("p (h e) -> p h e", h=4),
                                        st[d][:, bass.ds(slot_in(g, r, d), 256)].rearrange("p (h e) -> p h e", h=4),
                                        decay, ALU.mult).then_inc(order, 1)
            for d, g in enumerate(tiles):
                wait_apart(dve, order, i * 4 + (done + 3 + d), turns)
                out = st[d][:, bass.ds(slot_out(g, r, d), 256)]
                nc.vector.tensor_tensor(out, out, tmp[:, d], ALU.add).then_inc(order, 1)
        done += 4 * (hi - lo)


A_R, A_E, A_XDT, A_Y, A_CBM = 0, 2048, 4096, 5120, 8192


def ssd(core, A):
    nc, sem = core.nc, core.sem
    ct = A.at(A_CT, NT * P)
    st = [A.at(A_STF, 256 * (NT + 2)), A.at(A_STB, 256 * (NT + 2))]
    dt, dta = A.at(A_DTS, G16), A.at(A_DTA, G16)
    dec = A.at(A_DEC, 5, G16)
    z = A.at(A_Z, NT * DSSD)
    xnat, cb = A.at(A_XNAT, NT * DSSD), A.at(A_CB, NT * 256)
    mixT = A.at(A_MIX, 8, NT * P)
    r_sum = A.at(A_R, 2, NS, P)
    e = A.at(A_E, 2, NS, P)
    xdt = A.at(A_XDT, 2, NS, HP)
    y = A.at(A_Y, 5, DSSD)
    cbm = A.at(A_CBM, 2, 2, P)
    junk = A.at(A_TAIL, DSSD)
    ctz = [core.small(f"c_groups{j}", [P, 2, P]) for j in range(2)]
    ss, ln, rstd = (core.small(f"ssd_{n}", [P, 2]) for n in ("ss", "ln", "rstd"))
    r_done = [sem("seg_terms_f"), sem("seg_terms_b")]
    seg_mm, e_done, m_done, xdt_done, ctz_done = (sem(n) for n in ("seg_mm", "seg_exp", "m_done", "xdt_done", "c_groups_done"))
    off_mm, diag_mm, xd_done, gated = sem("y_off_mm"), sem("y_diag_mm"), sem("xd_done"), sem("y_gated")
    sq_done, rstd_done, normed, y_turned, mix_out = (sem(n) for n in ("y_sumsq", "y_rstd", "y_normed", "y_turned", "y_mix"))
    act_order, pool_turns = sem("ssd_act_order"), sem("ssd_pool_turns")
    heads = lambda t: t.rearrange("p (h e) -> p h e", h=NS)

    def terms(ops, eng, g, d):
        ops.tensor_tensor(r_sum[:, d], core.masks[:, (M_LE, M_GE)[d], :].unsqueeze(1).broadcast_to([P, NS, P]),
                          dta[:, bass.ds(g * 16 + 8 * d, 8)].unsqueeze(2).broadcast_to([P, NS, P]),
                          ALU.mult).then_inc(r_done[d], 1)

    with nc.Block() as block:
        @block.gpsimd
        def _(pool):
            def body(g, j, r):
                wait_apart(pool, seg_mm, g + 1, pool_turns)
                terms(nc.gpsimd, pool, g, 1)
                wait_apart(pool, diag_mm, g + 1, pool_turns)
                nc.gpsimd.tensor_tensor(xdt, heads(xnat[:, bass.ds(g * DSSD, DSSD)]).unsqueeze(1).broadcast_to([P, 2, NS, HP]),
                                        dt[:, bass.ds(g * 16, 16)].rearrange("p (d h) -> p d h", d=2).unsqueeze(3)
                                        .broadcast_to([P, 2, NS, HP]), ALU.mult).then_inc(xdt_done, 1)
                wait_apart(pool, gated, g + 1, pool_turns)
                nc.gpsimd.tensor_tensor(heads(y[:, 2]), heads(xnat[:, bass.ds(g * DSSD, DSSD)]),
                                        core.rows[:, ROW_D:ROW_D + 8].unsqueeze(2).broadcast_to([P, NS, HP]),
                                        ALU.mult).then_inc(xd_done, 1)
            tile_loop(pool, body)

        @block.scalar
        def _(act):
            act.preload_act_table_set("natural_log_exp_and_others")

            def body(g, j, r):
                act.wait_ge(seg_mm, g + 2)
                act.wait_ge(diag_mm, g + 1)
                for d in range(2):
                    for half in range(2):
                        nc.scalar.activation(e[:, d, 4 * half:4 * half + 4, :],
                                             core.ps[2 * d + half][:, :].rearrange("p (h q) -> p h q", h=4),
                                             ACT.Exp).then_inc(e_done, 1)
                act.wait_ge(gated, g + 2)
                for grp in range(2):
                    nc.scalar.activation(junk[:, 256 * grp:256 * grp + 256], y[:, 3, 256 * grp:256 * grp + 256],
                                         ACT.Square, accum_out=ss[:, grp:grp + 1]).then_inc(act_order, 1)
                act.wait_ge(act_order, g * 3 + 2)
                nc.scalar.activation(ln[:], ss[:], ACT.Ln, bias=core.eps[:, 0:1], scale=1.0 / 256).then_inc(act_order, 1)
                act.wait_ge(act_order, g * 3 + 3)
                nc.scalar.activation(rstd[:], ln[:], ACT.Exp, scale=-0.5).then_inc(rstd_done, 1)
                act.wait_ge(y_turned, g + 1)
                for c in range(4):
                    ins = nc.scalar.activation(mixT[:, 4 + c, bass.ds(g * P, P)], core.ps[7][:, c * P:(c + 1) * P],
                                               ACT.Copy, scale=core.col("ssd_norm", c))
                ins.then_inc(mix_out, 1)
            tile_loop(act, body)

        @block.vector
        def _(dve):
            dve.sem_inc(seg_mm, 1)
            dve.sem_inc(diag_mm, 1)
            dve.sem_inc(gated, 1)
            for t in ctz:
                nc.vector.memset(t[0:64, 1, :], 0.0)
                nc.vector.memset(t[64:128, 0, :], 0.0)

            def body(g, j, r):
                order = Order(dve, sem("ssd_dve_order"), g * 4)
                dve.wait_ge(seg_mm, g + 1)
                terms(nc.vector, dve, g, 0)
                nc.vector.tensor_copy(ctz[j][0:64, 0, :], ct[0:64, bass.ds(g * P, P)])
                nc.vector.tensor_copy(ctz[j][64:128, 1, :], ct[64:128, bass.ds(g * P, P)]).then_inc(ctz_done, 1)
                for d in range(2):
                    ins = nc.vector.tensor_tensor(
                        cbm[:, d], cb[:, bass.ds(g * 256, 256)].rearrange("p (a q) -> p a q", a=2),
                        core.masks[:, (M_LE, M_GE)[d], :].unsqueeze(1).broadcast_to([P, 2, P]), ALU.mult)
                order.link(ins)
                for d in range(2):
                    dve.wait_ge(e_done, g * 4 + (2 * d + 2))
                    v = e[:, d].rearrange("p (a h) q -> p a h q", a=2)
                    nc.vector.tensor_tensor(v, v, cbm[:, d].unsqueeze(2).broadcast_to([P, 2, 4, P]),
                                            ALU.mult).then_inc(m_done, 1)
                dve.wait_ge(off_mm, g + 1)
                for d in range(2):
                    nc.vector.tensor_tensor(
                        heads(y[:, d]), heads(core.ps[5 + d][:, :]),
                        dec[:, (D_CSF, D_CSB)[d], bass.ds(g * 16 + 8 * d, 8)].unsqueeze(2).broadcast_to([P, NS, HP]),
                        ALU.mult).then_inc(sem("y_off_done"), 1)
                dve.wait_ge(sem("y_off_done"), g * 2 + 2)
                order.link(nc.vector.tensor_tensor(y[:, 0], y[:, 0], y[:, 1], ALU.add))
                dve.wait_ge(xd_done, g + 1)
                order.link(nc.vector.tensor_tensor(y[:, 0], y[:, 0], y[:, 2], ALU.add))
                dve.wait_ge(diag_mm, g + 2)
                order.link(nc.vector.tensor_tensor(y[:, 0], y[:, 0], core.ps[4][:, :], ALU.add))
                nc.vector.tensor_tensor(y[:, 3], y[:, 0], z[:, bass.ds(g * DSSD, DSSD)], ALU.mult).then_inc(gated, 1)
                dve.wait_ge(rstd_done, g + 1)
                for grp in range(2):
                    ins = nc.vector.tensor_scalar(y[:, 4, 256 * grp:256 * grp + 256], y[:, 3, 256 * grp:256 * grp + 256],
                                                  rstd[:, grp:grp + 1], None, ALU.mult)
                ins.then_inc(normed, 1)
                assert order.n == 4
            tile_loop(dve, body)

        @block.tensor
        def _(pe):
            def body(g, j, r):
                for d in range(2):
                    pe.wait_ge(r_done[d], g + 1)
                    for half in range(2):
                        mm = nc.tensor.matmul(core.ps[2 * d + half][:, :], core.masks[:, (M_GT, M_LT)[d], :],
                                              r_sum[:, d, 4 * half:4 * half + 4, :].rearrange("p h q -> p (h q)"),
                                              start=True, stop=True)
                mm.then_inc(seg_mm, 1)
                pe.wait_ge(ctz_done, g + 1)
                for d in range(2):
                    for grp in range(2):
                        mm = nc.tensor.matmul(core.ps[5 + d][:, 256 * grp:256 * grp + 256], ctz[j][:, grp, :],
                                              st[d][:, bass.ds(slot_in(g, r, d), 256)], start=True, stop=True)
                mm.then_inc(off_mm, 1)
                pe.wait_ge(m_done, g * 2 + 2)
                pe.wait_ge(xdt_done, g + 1)
                for h in range(NS):
                    for d in range(2):
                        mm = nc.tensor.matmul(core.ps[4][:, h * HP:(h + 1) * HP], e[:, d, h, :], xdt[:, d, h, :],
                                              start=(d == 0), stop=(d == 1))
                mm.then_inc(diag_mm, 1)
                pe.wait_ge(normed, g + 1)
                for c in range(4):
                    mm = nc.tensor.transpose(core.ps[7][:, c * P:(c + 1) * P], y[:, 4, c * P:(c + 1) * P], core.ident)
                mm.then_inc(y_turned, 1)
            tile_loop(pe, body)


A_KT, A_WUQ, A_WUKV = 0, 8192, 9728
A_KN = 10752
A_V = A_DT
A_P, A_PT = A_V + 4096, A_V + 6144
A_QN, A_QT = A_V + 8192, A_V + 9728
A_O, A_CN, A_CT2 = A_V + 11776, A_V + 13824, A_V + 14592
A_ROT = A_V + 15360


def rope(nc, link, out1, out2, x1, x2, cos, sin, t):
    nc.vector.tensor_tensor(t[0], x1, cos, ALU.mult)
    nc.vector.tensor_tensor(t[1], x2, sin, ALU.mult)
    nc.vector.tensor_tensor(t[2], x2, cos, ALU.mult)
    link(nc.vector.tensor_tensor(t[3], x1, sin, ALU.mult))
    nc.vector.tensor_tensor(out1, t[0], t[1], ALU.subtract)
    return nc.vector.tensor_tensor(out2, t[2], t[3], ALU.add)


def keys(core, A, r):
    nc, io, sem = core.nc, core.io, core.sem
    nat = A.at(A_NAT, NT * NAT)
    kT = A.at(A_KT, NH, 1024)
    wuq, wukv = A.at(A_WUQ, 2, NH * DQK), A.at(A_WUKV, NH * (DN + DV))
    kn = [A.at(A_KN + 768 * j, NH, DQK) for j in range(2)]
    v = A.at(A_V, 4096)
    cn = [A.at(A_CN + 384 * j, 384) for j in range(2)]
    cT = [A.at(A_CT2 + 384 * j, 3, P) for j in range(2)]
    rot = [A.at(A_ROT + 16 * i, 16) for i in range(4)]
    ss, ln, rstd = (core.small(f"kv_{n}{r}", [P, 2]) for n in ("ss", "ln", "rstd"))
    junk = A.at(A_ROT + 64, P)
    order_a, rstd_done, cn_done = sem("kv_act_order"), sem("kv_rstd"), sem("ckv_normed")
    turned, cT_done, kv_mm, rot_order = sem("ckv_turned"), sem("ckvT_done"), sem("kv_mm"), sem("k_rot_order")
    kn_done, v_done, k_turned, kT_act, kT_dve = (sem(n) for n in ("kn_done", "v_done", "k_turned", "kT_act", "kT_dve"))

    with nc.Block() as block:
        if r == 0:
            @block.sync
            def _(sp):
                sp.dma_start(wuq, io["w_uq"][0].rearrange("(k p) n -> p k n", p=P)).then_inc(sem("w_qkv_in"), 16)
                sp.dma_start(wukv, io["w_ukv"][0]).then_inc(sem("w_qkv_in"), 16)

        @block.scalar
        def _(act):
            act.preload_act_table_set("natural_log_exp_and_others")

            def stats(g, i, j):
                nc.scalar.activation(junk, nat[:, bass.ds(g * NAT + QL, KVL)], ACT.Square,
                                     accum_out=ss[:, j:j + 1]).then_inc(order_a, 1)
                act.wait_ge(order_a, g * 2 + 1)
                nc.scalar.activation(ln[:, j:j + 1], ss[:, j:j + 1], ACT.Ln, bias=core.eps[:, 0:1],
                                     scale=1.0 / KVL).then_inc(order_a, 1)
                act.wait_ge(order_a, g * 2 + 2)
                nc.scalar.activation(rstd[:, j:j + 1], ln[:, j:j + 1], ACT.Exp, scale=-0.5).then_inc(rstd_done, 1)

            def turned_c(g, i, j):
                act.wait_ge(turned, g + 1)
                nc.scalar.activation(cT[j][:, 2, :], core.ps[0][:, 0:P], ACT.Copy,
                                     scale=core.col("kv_norm")).then_inc(cT_done, 1)

            def take_kv(g, i, j):
                act.wait_ge(kv_mm, g + 1)
                kv = core.ps[1].rearrange("p (h e) -> p h e", h=4)
                nc.scalar.activation(kn[j][:, 0:4, 0:DN], kv[:, :, 0:DN], ACT.Copy)
                nc.scalar.activation(v[:, bass.ds(i * 512, 256)].rearrange("p (h e) -> p h e", h=4), kv[:, :, DN:],
                                     ACT.Copy).then_inc(v_done, 1)

            def take_kT(g, i, j):
                act.wait_ge(k_turned, g + 1)
                nc.scalar.activation(kT[0:DQK, 0:4, bass.ds(i * P, P)],
                                     core.ps[3][0:DQK, :].rearrange("p (h t) -> p h t", h=4), ACT.Copy).then_inc(kT_act, 1)
            request_pipeline(act, r, [(0, take_kT), (1, take_kv), (2, turned_c), (3, stats)])

        @block.vector
        def _(dve):
            def norm(g, i, j):
                dve.wait_ge(rstd_done, g + 1)
                nc.vector.tensor_scalar(cn[j][:, QL:], nat[:, bass.ds(g * NAT + QL, KVL)], rstd[:, j:j + 1], None,
                                        ALU.mult).then_inc(cn_done, 1)

            def take_kv(g, i, j):
                order = Order(dve, rot_order, g)
                kr = nat[:, bass.ds(g * NAT + (QL + KVL), DR)]
                ropes = core.rope[:, bass.ds(i, 1)].rearrange("p o s f -> p (o s f)")
                spread = [t.unsqueeze(1).broadcast_to([P, NH, 16]) for t in rot]
                nc.vector.tensor_tensor(rot[0], kr[:, 0:16], ropes[:, 0:16], ALU.mult)
                nc.vector.tensor_tensor(rot[1], kr[:, 16:32], ropes[:, 16:32], ALU.mult)
                nc.vector.tensor_tensor(rot[2], kr[:, 16:32], ropes[:, 0:16], ALU.mult)
                order.link(nc.vector.tensor_tensor(rot[3], kr[:, 0:16], ropes[:, 16:32], ALU.mult))
                nc.vector.tensor_tensor(kn[j][:, :, DN:DN + 16], spread[0], spread[1], ALU.subtract)
                nc.vector.tensor_tensor(kn[j][:, :, DN + 16:], spread[2], spread[3], ALU.add)
                dve.wait_ge(kv_mm, g + 1)
                kv = core.ps[2].rearrange("p (h e) -> p h e", h=4)
                nc.vector.tensor_copy(kn[j][:, 4:8, 0:DN], kv[:, :, 0:DN])
                nc.vector.tensor_copy(v[:, bass.ds(i * 512 + 256, 256)].rearrange("p (h e) -> p h e", h=4),
                                      kv[:, :, DN:]).then_inc(kn_done, 1)

            def take_kT(g, i, j):
                dve.wait_ge(k_turned, g + 1)
                nc.vector.tensor_copy(kT[0:DQK, 4:8, bass.ds(i * P, P)],
                                      core.ps[4][0:DQK, :].rearrange("p (h t) -> p h t", h=4)).then_inc(kT_dve, 1)
            request_pipeline(dve, r, [(0, take_kT), (1, take_kv), (3, norm)])

        @block.tensor
        def _(pe):
            pe.wait_ge(sem("w_qkv_in"), 32)

            def turn_c(g, i, j):
                pe.wait_ge(cn_done, g + 1)
                nc.tensor.transpose(core.ps[0][:, 0:P], cn[j][:, QL:], core.ident).then_inc(turned, 1)

            def expand(g, i, j):
                pe.wait_ge(cT_done, g + 1)
                for half in range(2):
                    mm = nc.tensor.matmul(core.ps[1 + half], cT[j][:, 2, :], wukv[:, 512 * half:512 * half + 512],
                                          start=True, stop=True)
                mm.then_inc(kv_mm, 1)

            def turn_k(g, i, j):
                pe.wait_ge(kn_done, g + 1)
                pe.wait_ge(v_done, g + 1)
                for h in range(NH):
                    mm = nc.tensor.transpose(core.ps[3 + h // 4][0:DQK, h % 4 * P:(h % 4 + 1) * P], kn[j][:, h, :],
                                             core.ident)
                mm.then_inc(k_turned, 1)
            request_pipeline(pe, r, [(0, turn_k), (1, expand), (2, turn_c)])


Q_STATS, Q_TURN, Q_MM0, Q_MM1, Q_ROPE, Q_T0, Q_T1 = range(7)


def attention(core, A, r):
    nc, io, sem = core.nc, core.io, core.sem
    lo, hi = TILES[r]
    n_tiles = hi - lo
    keys_n = T_OF[r]
    nkt = keys_n // P
    nat = A.at(A_NAT, NT * NAT)
    kT = A.at(A_KT, NH, 1024)
    wuq = A.at(A_WUQ, 2, NH * DQK)
    v = A.at(A_V, 8, NH, DV)
    prob = [A.at(A_P + 1024 * b, 1024) for b in range(2)]
    probT = [A.at(A_PT + 1024 * b, 8, P) for b in range(2)]
    qn = [A.at(A_QN + 768 * j, NH, DQK) for j in range(2)]
    qT = [A.at(A_QT + 1024 * j, NH, P) for j in range(2)]
    o = [A.at(A_O + 1024 * j, 2, NH * DV) for j in range(2)]
    cn = [A.at(A_CN + 384 * j, 384) for j in range(2)]
    cT = [A.at(A_CT2 + 384 * j, 3, P) for j in range(2)]
    rot = [A.at(A_ROT + P * i, NH, 16) for i in range(4)]
    mixT = A.at(A_MIX, 8, NT * P)
    junk = A.at(A_ROT + 4 * P, 512)
    q_ss, q_ln, q_rstd, o_ss, o_ln, o_rstd, top, bias = (
        core.small(f"att_{n}{r}", [P, 2]) for n in ("q_ss", "q_ln", "q_rstd", "o_ss", "o_ln", "o_rstd", "top", "bias"))
    total = core.small(f"att_total{r}", [P, 2, NH])
    inv = core.small(f"att_inv{r}", [P, 2, NH])
    q_rstd_done, cq_normed, cq_turned, cqT_done, q_mm, q_copied, q_roped, q_turned, qT_done = (
        sem(n) for n in ("q_rstd", "cq_normed", "cq_turned", "cqT_done", "q_mm", "q_copied", "q_roped", "q_turned", "qT_done"))
    scored, topped, biased, exped, p_turned, pT_act, pT_dve, valued = (
        sem(n) for n in ("scored", "topped", "biased", "exped", "p_turned", "pT_act", "pT_dve", "valued"))
    o_done, o_rstd_done, o_normed, o_turned, o_mixed = (
        sem(n) for n in ("o_done", "o_rstd", "o_normed", "o_turned", "o_mixed"))
    act_order, o_order, dve_order, inv_done = sem("att_act_order"), sem("att_o_order"), sem("att_dve_order"), sem("att_inv")
    half = nkt // 2
    spare = core.ps[7]

    def tiles(eng, first, body, last):
        first()
        for j in range(2):
            body(lo + j, j, j, j == 1, True)
        if n_tiles > 4:
            with eng.Fori(1, n_tiles // 2 - 1) as turn:
                for j in range(2):
                    body(turn * 2 + (lo + j), turn * 2 + j, j, True, True)
        for j in range(2):
            body(hi - 2 + j, n_tiles - 2 + j, j, True, j == 0)
        last(hi - 1, 1)

    with nc.Block() as block:
        @block.scalar
        def _(act):
            act.preload_act_table_set("natural_log_exp_and_others")

            def front(step, g, i, j):
                if step == Q_STATS:
                    nc.scalar.activation(junk[:, 0:QL], nat[:, bass.ds(g * NAT, QL)], ACT.Square,
                                         accum_out=q_ss[:, j:j + 1]).then_inc(act_order, 1)
                    act.wait_ge(act_order, g * 2 + 1)
                    nc.scalar.activation(q_ln[:, j:j + 1], q_ss[:, j:j + 1], ACT.Ln, bias=core.eps[:, 0:1],
                                         scale=1.0 / QL).then_inc(act_order, 1)
                    act.wait_ge(act_order, g * 2 + 2)
                    nc.scalar.activation(q_rstd[:, j:j + 1], q_ln[:, j:j + 1], ACT.Exp, scale=-0.5).then_inc(q_rstd_done, 1)
                elif step == Q_TURN:
                    act.wait_ge(cq_turned, g + 1)
                    for k in range(2):
                        ins = nc.scalar.activation(cT[j][:, k, :], spare[:, k * P:(k + 1) * P], ACT.Copy,
                                                   scale=core.col("q_norm", k))
                    ins.then_inc(cqT_done, 1)
                elif step in (Q_MM0, Q_MM1):
                    part, h0, h1 = (0, 0, 5) if step == Q_MM0 else (1, 5, 8)
                    act.wait_ge(q_mm, g * 2 + (part + 1))
                    nc.scalar.activation(qn[j][:, h0:h1, :].rearrange("p h e -> p (h e)"),
                                         spare[:, 0:(h1 - h0) * DQK], ACT.Copy).then_inc(q_copied, 1)

            def exps(g, h, j):
                act.wait_ge(biased, g * NH + (h + 1))
                nc.scalar.activation(prob[h % 2][:, 0:keys_n], core.banks[:, h % 2 * 1024:h % 2 * 1024 + keys_n],
                                     ACT.Exp, bias=bias[:, h % 2:h % 2 + 1], scale=SCALE,
                                     accum_out=total[:, j, h:h + 1]).then_inc(exped, 1)

            def first():
                for step in range(7):
                    front(step, lo, 0, 0)
                exps(lo, 0, 0)

            def last(g, j):
                o_stats(g, j)
                mix(g, j)

            def body(g, i, j, before, more):
                for h in range(NH):
                    if h + 1 < NH:
                        exps(g, h + 1, j)
                    elif more:
                        exps(g + 1, 0, 1 - j)
                    act.wait_ge(p_turned, g * NH + (h + 1))
                    nc.scalar.activation(probT[h % 2][:, 0:half, :],
                                         core.banks[:, 2048:2048 + half * P].rearrange("p (k q) -> p k q", k=half),
                                         ACT.Copy).then_inc(pT_act, 1)
                    if more and h < 7:
                        front(h, g + 1, i + 1, 1 - j)
                    if before and h == 1:
                        o_stats(g - 1, 1 - j)
                    if before and h == 7:
                        mix(g - 1, 1 - j)

            def o_stats(g, j):
                act.wait_ge(o_done, g + 2)
                nc.scalar.activation(junk, o[j][:, 0, :], ACT.Square, accum_out=o_ss[:, j:j + 1]).then_inc(o_order, 1)
                act.wait_ge(o_order, g * 2 + 1)
                nc.scalar.activation(o_ln[:, j:j + 1], o_ss[:, j:j + 1], ACT.Ln, bias=core.eps[:, 0:1],
                                     scale=1.0 / (NH * DV)).then_inc(o_order, 1)
                act.wait_ge(o_order, g * 2 + 2)
                nc.scalar.activation(o_rstd[:, j:j + 1], o_ln[:, j:j + 1], ACT.Exp, scale=-0.5).then_inc(o_rstd_done, 1)

            def mix(g, j):
                act.wait_ge(o_turned, g + 1)
                for c in range(4):
                    ins = nc.scalar.activation(mixT[:, c, bass.ds(g * P, P)], spare[:, c * P:(c + 1) * P], ACT.Copy,
                                               scale=core.col("attn_norm", c))
                ins.then_inc(o_mixed, 1)
            tiles(act, first, body, last)

        @block.vector
        def _(dve):
            def front(step, g, i, j):
                if step == Q_STATS:
                    dve.wait_ge(q_rstd_done, g + 1)
                    nc.vector.tensor_scalar(cn[j][:, 0:QL], nat[:, bass.ds(g * NAT, QL)], q_rstd[:, j:j + 1], None,
                                            ALU.mult).then_inc(cq_normed, 1)
                elif step == Q_ROPE:
                    order = Order(dve, dve_order, g)
                    dve.wait_ge(q_copied, g * 2 + 2)
                    ropes = core.rope[:, bass.ds(i, 1)].rearrange("p o s f -> p (o s) f")
                    cos, sin = (ropes[:, s:s + 1, :].broadcast_to([P, NH, 16]) for s in range(2))
                    x1, x2 = qn[j][:, :, DN:DN + 16], qn[j][:, :, DN + 16:]
                    rope(nc, order.link, x1, x2, x1, x2, cos, sin, rot).then_inc(q_roped, 1)
                elif step in (Q_T0, Q_T1):
                    part = step - Q_T0
                    dve.wait_ge(q_turned, g * 2 + (part + 1))
                    nc.vector.tensor_copy(qT[j][0:DQK, 4 * part:4 * part + 4, :],
                                          spare[0:DQK, :].rearrange("p (h t) -> p h t", h=4)).then_inc(qT_done, 1)

            def tops(g, h):
                dve.wait_ge(scored, g * NH + (h + 1))
                nc.vector.tensor_reduce(top[:, h % 2:h % 2 + 1], core.banks[:, h % 2 * 1024:h % 2 * 1024 + keys_n],
                                        AX_X, ALU.max).then_inc(topped, 1)
                dve.wait_ge(topped, g * NH + (h + 1))
                nc.vector.tensor_scalar(bias[:, h % 2:h % 2 + 1], top[:, h % 2:h % 2 + 1], -SCALE, None,
                                        ALU.mult).then_inc(biased, 1)

            def first():
                if r == 0:
                    dve.sem_inc(pT_dve, 1)
                    dve.sem_inc(pT_act, 1)
                    dve.sem_inc(o_done, 1)
                for step in range(7):
                    front(step, lo, 0, 0)
                tops(lo, 0)

            def last(g, j):
                divide(g, j)
                norm(g, j)

            def body(g, i, j, before, more):
                for h in range(NH):
                    if h + 1 < NH:
                        tops(g, h + 1)
                    elif more:
                        tops(g + 1, 0)
                    dve.wait_ge(p_turned, g * NH + (h + 1))
                    nc.vector.tensor_copy(probT[h % 2][:, half:nkt, :],
                                          core.banks[:, 2560:2560 + half * P].rearrange("p (k q) -> p k q", k=half)
                                          ).then_inc(pT_dve, 1)
                    if before and h == 0:
                        divide(g - 1, 1 - j)
                    if before and h == 2:
                        norm(g - 1, 1 - j)
                    if more and h < 7:
                        front(h, g + 1, i + 1, 1 - j)

            def divide(g, j):
                dve.wait_ge(valued, g + 1)
                nc.vector.reciprocal(inv[:, j], total[:, j]).then_inc(inv_done, 1)
                dve.wait_ge(inv_done, g + 1)
                nc.vector.tensor_tensor(o[j][:, 0].rearrange("p (h e) -> p h e", h=NH),
                                        core.ps[6].rearrange("p (h e) -> p h e", h=NH),
                                        inv[:, j].unsqueeze(2).broadcast_to([P, NH, DV]), ALU.mult).then_inc(o_done, 1)

            def norm(g, j):
                dve.wait_ge(o_rstd_done, g + 1)
                nc.vector.tensor_scalar(o[j][:, 1], o[j][:, 0], o_rstd[:, j:j + 1], None, ALU.mult).then_inc(o_normed, 1)
            tiles(dve, first, body, last)

        @block.tensor
        def _(pe):
            def front(step, g, i, j):
                if step == Q_TURN:
                    pe.wait_ge(cq_normed, g + 1)
                    for k in range(2):
                        mm = nc.tensor.transpose(spare[:, k * P:(k + 1) * P], cn[j][:, k * P:(k + 1) * P], core.ident)
                    mm.then_inc(cq_turned, 1)
                elif step in (Q_MM0, Q_MM1):
                    part, h0, h1 = (0, 0, 5) if step == Q_MM0 else (1, 5, 8)
                    if part:
                        pe.wait_ge(q_copied, g * 2 + 1)
                    else:
                        pe.wait_ge(cqT_done, g + 1)
                    for k in range(2):
                        mm = nc.tensor.matmul(spare[:, 0:(h1 - h0) * DQK], cT[j][:, k, :],
                                              wuq[:, k, h0 * DQK:h1 * DQK], start=(k == 0), stop=(k == 1))
                    mm.then_inc(q_mm, 1)
                elif step in (Q_T0, Q_T1):
                    part = step - Q_T0
                    if part:
                        pe.wait_ge(qT_done, g * 2 + 1)
                    else:
                        pe.wait_ge(q_roped, g + 1)
                    for h in range(4):
                        mm = nc.tensor.transpose(spare[0:DQK, h * P:(h + 1) * P], qn[j][:, 4 * part + h, :], core.ident)
                    mm.then_inc(q_turned, 1)

            def scores(g, h, j):
                pe.wait_ge(qT_done, g * 2 + 2)
                for k0 in range(0, keys_n, 512):
                    mm = nc.tensor.matmul(core.banks[:, h % 2 * 1024 + k0:h % 2 * 1024 + k0 + 512],
                                          qT[j][0:DQK, h, :], kT[0:DQK, h, k0:k0 + 512], start=True, stop=True)
                mm.then_inc(scored, 1)

            def values(g, h):
                for k in range(nkt):
                    mm = nc.tensor.matmul(core.ps[6][:, h * DV:(h + 1) * DV], probT[h % 2][:, k, :], v[:, k, h, :],
                                          start=(k == 0), stop=(k == nkt - 1))
                return mm

            def first():
                for step in range(7):
                    front(step, lo, 0, 0)
                scores(lo, 0, 0)

            def body(g, i, j, before, more):
                for h in range(NH):
                    if h + 1 < NH:
                        scores(g, h + 1, j)
                    elif more:
                        scores(g + 1, 0, 1 - j)
                    pe.wait_ge(exped, g * NH + (h + 1))
                    pe.wait_ge(pT_act, g * NH + (h + 1))
                    pe.wait_ge(pT_dve, g * NH + (h + 1))
                    for k in range(nkt):
                        at = 2048 + 512 * (k // half) + k % half * P
                        mm = nc.tensor.transpose(core.banks[:, at:at + P],
                                                 prob[h % 2][:, k * P:(k + 1) * P], core.ident)
                    mm.then_inc(p_turned, 1)
                    if h == 1:
                        pe.wait_ge(o_done, g + 1)
                    if h:
                        values(g, h - 1)
                    elif before:
                        values(g - 1, NH - 1).then_inc(valued, 1)
                    if more and h < 7:
                        front(h, g + 1, i + 1, 1 - j)
                    if before and h == 7:
                        turn_o(g - 1, 1 - j)

            def last(g, j):
                pe.wait_ge(pT_act, g * NH + (NH + 1))
                pe.wait_ge(pT_dve, g * NH + (NH + 1))
                values(g, NH - 1).then_inc(valued, 1)
                turn_o(g, j)

            def turn_o(g, j):
                pe.wait_ge(o_normed, g + 1)
                for c in range(4):
                    mm = nc.tensor.transpose(spare[:, c * P:(c + 1) * P], o[j][:, 1, c * P:(c + 1) * P], core.ident)
                mm.then_inc(o_turned, 1)
            tiles(pe, first, body, last)


def attend(core, A):
    for r in range(2):
        keys(core, A, r)
        attention(core, A, r)


A_WO, A_MT, A_WR = 0, 8192, 10240
A_OX = A_DT
A_GROW = A_OX + 9216
A_AFF = A_GROW + 2048


def row_of(nc, bank, columns, k, request, ident):
    return nc.tensor.matmul(bank[:, k % 4 * P:(k % 4 + 1) * P], columns.broadcast_to([P, P]), ident,
                            start=True, stop=True)


def output(core, A):
    nc, io, sem = core.nc, core.io, core.sem
    mixT = A.at(A_MIX, 8, NT * P)
    wo, wr = A.at(A_WO, 8, D), A.at(A_WR, KD, NE)
    mt = [A.at(A_MT + D * j, 8, P) for j in range(2)]
    x, x2, xn = ([A.at(A_OX + D * (2 * b + j), D) for j in range(2)] for b in range(3))
    hT = [A.at(A_OX + D * (6 + j), KD, P) for j in range(2)]
    junk = A.at(A_OX + 8 * D, D)
    gate_row = A.at(A_GROW, 2, D)
    aff = core.aff = A.at(A_AFF, 1024)
    ss, ln, rstd, top, total, inv = (core.small(f"out_{n}", [P, 2]) for n in ("ss", "ln", "rstd", "top", "total", "inv"))
    soft = [core.small(f"soft_aff{j}", [P, 2, NE]) for j in range(2)]
    x_in = [sem(f"out_x_in{j}") for j in range(2)]
    res_out, normed_out = ([sem(f"{n}{j}") for j in range(2)] for n in ("residual_out", "normed_out"))
    rows_mm, rows_done, mt_done, proj_mm, gated, x2_done = (
        sem(n) for n in ("gate_rows_mm", "gate_rows", "mt_done", "out_mm", "out_gated", "x2_done"))
    act_order, rstd_done, xn_done, turned, hT_act, hT_dve = (
        sem(n) for n in ("out_act_order", "out_rstd", "out_xn", "out_turned", "h2T_act", "h2T_dve"))
    logits, topped, exped, inv_done, soft_done, aff_turned, aff_done = (
        sem(n) for n in ("logits", "logit_top", "logit_exp", "logit_inv", "soft_done", "aff_turned", "aff_done"))
    x_of = (io["x_prompt"], io["x_sample"])

    with nc.Block() as block:
        @block.sync
        def _(sp):
            sp.dma_start(wo, io["w_out"][0].rearrange("(k p) n -> p k n", p=P)).then_inc(sem("w_out_in"), 16)
            sp.dma_start(wr, io["w_router"][0].rearrange("(k p) n -> p k n", p=P)).then_inc(sem("w_out_in"), 16)

            def front(g, j, r):
                sp.wait_ge(x2_done, g + 1)
                load_tile(sp, x[j], x_of, g, r, x_in[j])

            def back(g, j, r):
                sp.wait_ge(x2_done, g + 3)
                sp.dma_start(core.residual[bass.ds(g * P, P), :], x2[j]).then_inc(res_out[j], 16)
                sp.wait_ge(xn_done, g + 1)
                sp.dma_start(core.normed[bass.ds(g * P, P), :], xn[j]).then_inc(normed_out[j], 16)
            tile_pipeline(sp, [(0, front), (-1, back)])
            for j in range(2):
                sp.wait_ge(res_out[j], NT // 2 * 16)
                sp.wait_ge(normed_out[j], NT // 2 * 16)

        @block.scalar
        def _(act):
            act.preload_act_table_set("natural_log_exp_and_others")

            def stats(g, j, r):
                act.wait_ge(x2_done, g + 3)
                nc.scalar.activation(junk, x2[j], ACT.Square, accum_out=ss[:, j:j + 1]).then_inc(act_order, 1)
                act.wait_ge(act_order, g * 2 + 1)
                nc.scalar.activation(ln[:, j:j + 1], ss[:, j:j + 1], ACT.Ln, bias=core.eps[:, 0:1],
                                     scale=1.0 / D).then_inc(act_order, 1)
                act.wait_ge(act_order, g * 2 + 2)
                nc.scalar.activation(rstd[:, j:j + 1], ln[:, j:j + 1], ACT.Exp, scale=-0.5).then_inc(rstd_done, 1)

            def shift(g, j, r):
                act.wait_ge(turned, g + 1)
                for k in range(4):
                    ins = nc.scalar.activation(hT[j][:, k, :], core.ps[2][:, k * P:(k + 1) * P], ACT.Identity,
                                               bias=core.mod[:, 3 * KD + k, r:r + 1], scale=core.scale2[:, k, r:r + 1])
                ins.then_inc(hT_act, 1)

            def exp(g, j, r):
                act.wait_ge(topped, g * 2 + 2)
                nc.scalar.activation(soft[j][:, 0], core.ps[4][:, 0:NE], ACT.Exp, bias=top[:, j:j + 1],
                                     accum_out=total[:, j:j + 1]).then_inc(exped, 1)
            tile_pipeline(act, [(-2, exp), (-1, stats), (-1, shift)])

        @block.vector
        def _(dve):
            dve.sem_inc(x2_done, 2)
            nc.vector.memset(aff[0:48, :], -1.0)
            for r in range(2):
                for half in range(2):
                    dve.wait_ge(rows_mm, 2 * r + half + 1)
                    nc.vector.tensor_copy(gate_row[:, r, 512 * half:512 * half + 512], core.ps[half]).then_inc(rows_done, 1)

            def take(g, j, r):
                nc.vector.tensor_copy(mt[j], mixT[:, :, bass.ds(g * P, P)]).then_inc(mt_done, 1)

            def residual(g, j, r):
                if isinstance(g, int) and g == 0:
                    dve.wait_ge(rows_done, 4)
                if isinstance(g, int) and g < 2:
                    pass
                else:
                    dve.wait_ge(res_out[j], (g - j) * 8)
                dve.wait_ge(proj_mm, g * 2 + 2)
                for half in range(2):
                    ins = nc.vector.tensor_tensor(x2[j][:, 512 * half:512 * half + 512], core.ps[6 * j + half],
                                                  gate_row[:, r, 512 * half:512 * half + 512], ALU.mult)
                ins.then_inc(gated, 1)
                dve.wait_ge(x_in[j], (g - j) * 8 + 16)
                dve.wait_ge(gated, g + 1)
                nc.vector.tensor_tensor(x2[j], x2[j], x[j], ALU.add).then_inc(x2_done, 1)

            def norm(g, j, r):
                dve.wait_ge(rstd_done, g + 1)
                if isinstance(g, int) and g < 2:
                    pass
                else:
                    wait_apart(dve, normed_out[j], (g - j) * 8, sem("out_dve_turns"))
                nc.vector.tensor_scalar(xn[j], x2[j], rstd[:, j:j + 1], None, ALU.mult).then_inc(xn_done, 1)

            def shift(g, j, r):
                dve.wait_ge(turned, g + 1)
                for k in range(4, KD):
                    ins = nc.vector.tensor_scalar(hT[j][:, k, :], core.ps[3][:, (k - 4) * P:(k - 3) * P],
                                                  core.scale2[:, k, r:r + 1], core.mod[:, 3 * KD + k, r:r + 1],
                                                  ALU.mult, ALU.add)
                ins.then_inc(hT_dve, 1)

            def top_logit(g, j, r):
                dve.wait_ge(logits, g + 1)
                nc.vector.tensor_reduce(inv[:, j:j + 1], core.ps[4][:, 0:NE], AX_X, ALU.max).then_inc(topped, 1)
                dve.wait_ge(topped, g * 2 + 1)
                nc.vector.tensor_scalar(top[:, j:j + 1], inv[:, j:j + 1], -1.0, None, ALU.mult).then_inc(topped, 1)

            def softmax(g, j, r):
                dve.wait_ge(exped, g + 1)
                nc.vector.reciprocal(inv[:, j:j + 1], total[:, j:j + 1]).then_inc(inv_done, 1)
                dve.wait_ge(inv_done, g + 1)
                nc.vector.tensor_scalar(soft[j][:, 1], soft[j][:, 0], inv[:, j:j + 1], None, ALU.mult).then_inc(soft_done, 1)

            def affinities(g, j, r):
                dve.wait_ge(aff_turned, g + 1)
                nc.vector.tensor_copy(aff[32 * r:32 * r + NE, bass.ds((g - TILES[r][0]) * P, P)],
                                      core.ps[5][0:NE, 0:P]).then_inc(aff_done, 1)
            tile_pipeline(dve, [(-2, top_logit), (-1, residual), (-2, softmax), (-1, norm), (-1, shift),
                                (-2, affinities), (1, take)])

        @block.tensor
        def _(pe):
            for r in range(2):
                for half in range(2):
                    if r:
                        pe.wait_ge(rows_done, half + 1)
                    for k in range(4 * half, 4 * half + 4):
                        mm = row_of(nc, core.ps[half], core.mod[:, 2 * KD + k, r:r + 1], k, r, core.ident)
                    mm.then_inc(rows_mm, 1)
            pe.wait_ge(sem("w_out_in"), 32)
            pe.wait_ge(rows_done, 4)

            def project(half, g, j):
                for k in range(8):
                    mm = nc.tensor.matmul(core.ps[6 * j + half], mt[j][:, k, :], wo[:, k, 512 * half:512 * half + 512],
                                          start=(k == 0), stop=(k == 7))
                mm.then_inc(proj_mm, 1)

            def first_half(g, j, r):
                pe.wait_ge(mt_done, g + 1)
                pe.wait_ge(x2_done, g + 1)
                project(0, g, j)

            def second_half(g, j, r):
                project(1, g, j)

            def turn(g, j, r):
                pe.wait_ge(xn_done, g + 1)
                for k in range(KD):
                    mm = nc.tensor.transpose(core.ps[2 + k // 4][:, k % 4 * P:(k % 4 + 1) * P],
                                             xn[j][:, k * P:(k + 1) * P], core.ident)
                mm.then_inc(turned, 1)

            def route(g, j, r):
                pe.wait_ge(hT_act, g + 1)
                pe.wait_ge(hT_dve, g + 1)
                for k in range(KD):
                    mm = nc.tensor.matmul(core.ps[4][:, 0:NE], hT[j][:, k, :], wr[:, k, :],
                                          start=(k == 0), stop=(k == KD - 1))
                mm.then_inc(logits, 1)

            def turn_soft(g, j, r):
                pe.wait_ge(soft_done, g + 1)
                nc.tensor.transpose(core.ps[5][0:NE, 0:P], soft[j][:, 1], core.ident).then_inc(aff_turned, 1)
            tile_pipeline(pe, [(0, first_half), (-2, turn_soft), (-1, turn), (0, second_half), (-1, route)])


def choice(core, A):
    nc, sem = core.nc, core.sem
    left = [A.at(A_AFF, 1024)[0:48, :], A.at(0, 1024)[0:48, :]]
    best = A.at(1024, CAP[1])[0:48, :]
    place = A.at(1152, CAP[1])[0:48, :]
    places = core.small("places", [48, CAP[1]], U32)
    ranked, turned = sem("choice_order"), sem("choice_turned")

    with nc.Block() as block:
        @block.vector
        def _(dve):
            order = Order(dve, ranked)
            for n in range(CAP[1] // 8):
                eight = slice(8 * n, 8 * n + 8)
                now, then = left[n % 2], left[1 - n % 2]
                order.link(nc.vector.max(best[:, eight], now))
                nc.vector.max_index(places[:, eight], best[:, eight], now)
                order.link(nc.vector.match_replace(then, best[:, eight], now, -2.0))
            nc.vector.tensor_copy(place[0:32], places[0:32, :])
            order.link(nc.vector.tensor_scalar(place[32:48], places[32:48, :], float(T_OF[0]), None, ALU.add))
            dve.sem_inc(sem("choice_ready"), 1)
            dve.wait_ge(turned, 1)
            nc.vector.tensor_copy(core.chosen[:], core.ps[0][:, 0:48])
            nc.vector.tensor_copy(core.gates[:], core.ps[0][:, 64:112])

        @block.tensor
        def _(pe):
            pe.wait_ge(sem("choice_ready"), 1)
            nc.tensor.transpose(core.ps[0][:, 0:48], place, core.ident[0:48, 0:48])
            nc.tensor.transpose(core.ps[0][:, 64:112], best, core.ident[0:48, 0:48]).then_inc(turned, 1)


CT = sum(CAP)
SPLIT = ((1, 0, CAP[1]), (0, CAP[1], CT))
FS = FE // 512
UNITS = [(kind, fc) for fc in range(4) for kind in (0, 1)] + [(2, fc) for fc in range(4)]
NU = len(UNITS)
PAIRS = [(kind, half) for half in range(2) for kind in (0, 1)] + [(2, 0), (2, 1)]
LEAD, LEAD_HIGH = 8, 10
F32R = mybir.dt.float32r


def experts(core, A):
    nc, io, sem = core.nc, core.io, core.sem
    raw = [core.small(f"slab_{kind}", [P, KD * 512]) for kind in ("gate", "up", "down")]
    w_hi, w_lo = (core.small(f"weights_{n}", [P, NU, 1024], F32R) for n in ("high", "low"))
    xe = [core.small(f"rows{b}", [CAP[r], D]) for b, r in enumerate((1, 0))]
    y = [core.small(f"weighted{b}", [CAP[r], D]) for b, r in enumerate((1, 0))]
    gain = core.small("gain_rows", [P, 2, D])
    xT = core.small("rowsT", [P, KD, CT])
    x = core.small("rowsT_parts", [P, KD, 2 * CT], F32R)
    h = core.small("hidden", [P, 2, CT])
    h_parts = core.small("hidden_parts", [P, 4, 2 * CT], F32R)
    sample_hi, prompt_hi, prompt_pair, sample_lo = (slice(*s) for s in (
        (0, CAP[1]), (CAP[1], CT), (CAP[1], CT + CAP[0]), (CT + CAP[0], 2 * CT)))
    sums = core.small("gate_up_sums", [P, 2, 2, CT])
    sil = core.small("silu_gate", [P, 2, CT])
    rows_in = [core.small(f"rows_in{b}", [CAP[r], 1], U32) for b, r in enumerate((1, 0))]
    rows_out = [core.small(f"rows_out{b}", [CAP[r], 1], U32) for b, r in enumerate((1, 0))]
    pair_in = [[sem(f"pair_{kind}{half}_in") for half in range(2)] for kind in ("gate", "up", "down")]
    unit_hi, unit_lo, unit_used = sem("unit_high"), sem("unit_low"), sem("unit_used")
    xe_in, y_out = ([sem(f"{n}{b}") for b in range(2)] for n in ("xe_in", "y_scattered"))
    rows_copied, gain_mm, gain_done = sem("rows_copied"), sem("gain_rows_mm"), sem("gain_rows")
    x_turned, xT_act, xT_dve, x_split = sem("xe_turned"), sem("xeT_act"), sem("xeT_dve"), sem("xeT_split")
    low_out, sum_done, sil_done, hid_done, hid_order = (sem(n) for n in ("gate_up_low", "gate_up_sum", "silu_gate", "hid_done", "hidden_order"))
    low_copied, low_added, y_done = sem("prompt_low_copied"), sem("prompt_low_added"), [sem(f"y_weighted{b}") for b in range(2)]
    dve_turns = sem("experts_dve_turns")
    y_banks = [core.banks[:, 2048 + 1024 * b:3072 + 1024 * b] for b in range(2)]
    STEPS = 4 * FS
    TURN0, TURNS = 8, 6

    def is_first(e, n=0):
        return isinstance(e, int) and e <= n

    def unit_of(slabs, n):
        kind, fc = UNITS[n]
        if kind == 2:
            return slabs[2][:, 1024 * fc:1024 * fc + 1024]
        return slabs[kind][:].rearrange("p (k n) -> p k n", k=KD)[:, :, P * fc:P * fc + P]

    def like(n, t):
        return t[:, n, :] if UNITS[n][0] == 2 else t[:, n, :].rearrange("p (k n) -> p k n", k=KD)

    def spare(s, kind):
        return core.ps[2 * (s % 2) + kind][:, 2 * CT:2 * CT + P]

    def turned(s, kind):
        b = 0 if s < 4 else 1
        r, c0, c1 = SPLIT[b]
        ks = [s + 4 * kind] if b == 0 else [2 * (s - 4) + 4 * kind + i for i in range(2)]
        return b, [(k, r, i * (c1 - c0), c0, c1) for i, k in enumerate(ks)]

    with nc.Block() as block:
        @block.sync
        def _(sp):
            views = (io["w_gate"][0].rearrange("e (k p) n -> p e k n", p=P),
                     io["w_up"][0].rearrange("e (k p) n -> p e k n", p=P),
                     io["w_down"][0].rearrange("e (k p) n -> p e k n", p=P))

            def load(e, fs):
                for kind, half in PAIRS:
                    if not (is_first(e) and fs == 0):
                        last = UNITS.index((kind, 2 * half + 1))
                        sp.wait_ge(unit_lo, e * (FS * NU) + ((fs - 1) * NU + last + 1))
                    src = views[kind][:, bass.ds(e, 1)] if not isinstance(e, int) else views[kind][:, e:e + 1]
                    if kind == 2:
                        src = src[:, :, 4 * fs + 2 * half:4 * fs + 2 * half + 2, :]
                        dst = raw[2][:, 2048 * half:2048 * half + 2048].rearrange("p (k n) -> p k n", k=2)
                    else:
                        at = 512 * fs + 256 * half
                        src = src[:, :, :, at:at + 256]
                        dst = raw[kind][:].rearrange("p (k n) -> p k n", k=KD)[:, :, 256 * half:256 * half + 256]
                    sp.dma_start(dst, src.rearrange("p e k n -> p (e k) n")).then_inc(pair_in[kind][half], 16)
            for fs in range(FS):
                load(0, fs)
            with sp.Fori(1, NE) as e:
                for fs in range(FS):
                    load(e, fs)

        @block.gpsimd
        def _(pool):
            def gather(e):
                for b, (r, _, _) in enumerate(SPLIT):
                    nc.gpsimd.tensor_copy(rows_in[b][:], core.chosen[0:CAP[r], bass.ds(e + 32 * r, 1)]).then_inc(rows_copied, 1)
                wait_apart(pool, rows_copied, 2 if is_first(e) else e * 4, sem("experts_pool_turns"))
                for b in range(2):
                    nc.gpsimd.indirect_dma_start(xe[b][:], None, core.normed, bass.IndirectOffsetOnAxis(ap=rows_in[b][:, 0:1], axis=0)
                                                 ).then_inc(xe_in[b], 16)

            def scatter(e):
                if not is_first(e):
                    for b in range(2):
                        wait_apart(pool, y_out[b], e * 16, sem("experts_pool_turns"))
                for b, (r, _, _) in enumerate(SPLIT):
                    ins = nc.gpsimd.tensor_copy(rows_out[b][:], core.chosen[0:CAP[r], bass.ds(e + 32 * r, 1)])
                    ins.then_inc(rows_copied, 1)
                pool.wait_ge(rows_copied, 4 * NE if isinstance(e, int) and e == NE - 1 else e * 4 + 6)
                for b in range(2):
                    wait_apart(pool, y_done[b], e + 1, sem("experts_pool_turns"))
                    nc.gpsimd.indirect_dma_start(core.residual, bass.IndirectOffsetOnAxis(ap=rows_out[b][:, 0:1], axis=0),
                                                 y[b][:], None, compute_op=ALU.add).then_inc(y_out[b], 16)

            def turn(e, more):
                if more:
                    wait_apart(pool, x_turned, e * TURNS + TURNS, sem("experts_pool_turns"))
                    gather(e + 1)
                scatter(e)
            gather(0)
            turn(0, True)
            with pool.Fori(1, NE - 1) as e:
                turn(e, True)
            turn(NE - 1, False)
            for b in range(2):
                pool.wait_ge(y_out[b], NE * 16)

        @block.scalar
        def _(act):
            def split(e, fs, n):
                kind, fc = UNITS[n]
                if fc % 2 == 0:
                    act.wait_ge(pair_in[kind][fc // 2], e * (16 * FS) + 16 * (fs + 1))
                if not (is_first(e) and fs == 0):
                    act.wait_ge(unit_used, e * (FS * NU) + ((fs - 1) * NU + n + 1))
                nc.scalar.activation(like(n, w_hi), unit_of(raw, n), ACT.Copy).then_inc(unit_hi, 1)

            def drain_x(e, s):
                act.wait_ge(x_turned, e * TURNS + (s + 1))
                for k, r, at, c0, c1 in turned(s, 0)[1]:
                    ins = nc.scalar.activation(xT[:, k, c0:c1], spare(s, 0)[:, at:at + c1 - c0], ACT.Identity,
                                               scale=core.scale2[:, k, r:r + 1], bias=core.mod[:, 3 * KD + k, r:r + 1])
                ins.then_inc(xT_act, 1)

            def copy_low(e):
                if not is_first(e):
                    act.wait_ge(y_out[1], e * 16)
                act.wait_ge(unit_used, e * (FS * NU) + FS * NU)
                nc.scalar.activation(y[1][:], y_banks[1][CAP[0]:2 * CAP[0], :], ACT.Copy).then_inc(low_copied, 1)

            def body(e, before, after):
                for n in range(FS * NU):
                    fs, u = divmod(n, NU)
                    kind, fc = UNITS[u]
                    step = 4 * fs + fc
                    if kind < 2:
                        act.wait_ge(unit_used, e * (FS * NU) + (n + 1))
                        nc.scalar.activation(sums[:, kind, fc % 2], core.ps[2 * (fc % 2) + kind][:, CT:2 * CT],
                                             ACT.Copy).then_inc(low_out, 1)
                    if kind == 0:
                        if after and 0 <= step - TURN0 < TURNS:
                            act.wait_ge(sum_done, e * (2 * STEPS) + (2 * step + 1))
                            drain_x(e + 1, step - TURN0)
                        act.wait_ge(sum_done, e * (2 * STEPS) + (2 * step + 1))
                        nc.scalar.activation(sil[:, fc % 2], sums[:, 0, fc % 2], ACT.Silu).then_inc(sil_done, 1)
                    if n + LEAD_HIGH < FS * NU:
                        split(e, (n + LEAD_HIGH) // NU, (n + LEAD_HIGH) % NU)
                    elif after:
                        split(e + 1, 0, (n + LEAD_HIGH) % NU)
                    if before and n == 0:
                        copy_low(e - 1)

            for s in range(TURNS):
                drain_x(0, s)
            for n in range(LEAD_HIGH):
                split(0, 0, n)
            body(0, False, True)
            body(1, True, True)
            with act.Fori(2, NE - 1) as e:
                body(e, True, True)
            body(NE - 1, True, False)
            copy_low(NE - 1)

        @block.vector
        def _(dve):
            def split(e, fs, n):
                dve.wait_ge(unit_hi, e * (FS * NU) + (fs * NU + n + 1))
                nc.vector.tensor_tensor(like(n, w_lo), unit_of(raw, n), like(n, w_hi[:].bitcast(F32)),
                                        ALU.subtract).then_inc(unit_lo, 1)

            def drain_x(e, s):
                dve.wait_ge(x_turned, e * TURNS + (s + 1))
                for k, r, at, c0, c1 in turned(s, 1)[1]:
                    ins = nc.vector.tensor_scalar(xT[:, k, c0:c1], spare(s, 1)[:, at:at + c1 - c0],
                                                  core.scale2[:, k, r:r + 1], core.mod[:, 3 * KD + k, r:r + 1],
                                                  ALU.mult, ALU.add)
                ins.then_inc(xT_dve, 1)

            def split_x(e):
                if not is_first(e):
                    dve.wait_ge(unit_used, e * (FS * NU) - (NU - UNITS.index((1, 3)) - 1))
                dve.wait_ge(xT_act, e * TURNS + TURNS)
                dve.wait_ge(xT_dve, e * TURNS + TURNS)
                nc.vector.tensor_copy(x[:, :, 0:CT], xT[:]).then_inc(x_split, 1)
                dve.wait_ge(x_split, e * 2 + 1)
                nc.vector.tensor_tensor(x[:, :, CT:2 * CT], xT[:], x[:, :, 0:CT].bitcast(F32), ALU.subtract).then_inc(x_split, 1)

            def weigh(e, b):
                r, _, _ = SPLIT[b]
                n = CAP[r]
                gates = core.gates[0:n, bass.ds(e + 32 * r, 1)]
                if b == 0:
                    if not is_first(e):
                        dve.wait_ge(y_out[0], e * 16)
                    wait_apart(dve, unit_used, e * (FS * NU) + FS * NU, dve_turns)
                    sums_of = y_banks[0]
                else:
                    dve.wait_ge(low_copied, e + 1)
                    nc.vector.tensor_tensor(y[1][:], y_banks[1][0:n, :], y[1][:], ALU.add).then_inc(low_added, 1)
                    wait_apart(dve, low_added, e + 1, dve_turns)
                    sums_of = y[1][:]
                nc.vector.scalar_tensor_tensor(out=y[b][:], in0=sums_of, scalar=gates, in1=gain[0:n, r, :],
                                               op0=ALU.mult, op1=ALU.mult).then_inc(y_done[b], 1)

            def body(e, before, after):
                for n in range(FS * NU):
                    fs, u = divmod(n, NU)
                    kind, fc = UNITS[u]
                    step = 4 * fs + fc
                    if kind < 2:
                        dve.wait_ge(low_out, e * (2 * STEPS) + (2 * step + kind + 1))
                        nc.vector.tensor_tensor(sums[:, kind, fc % 2], core.ps[2 * (fc % 2) + kind][:, 0:CT],
                                                sums[:, kind, fc % 2], ALU.add).then_inc(sum_done, 1)
                    if kind == 1:
                        if after and 0 <= step - TURN0 < TURNS:
                            drain_x(e + 1, step - TURN0)
                        dve.wait_ge(sil_done, e * STEPS + (step + 1))
                        dve.wait_ge(sum_done, e * (2 * STEPS) + (2 * step + 2))
                        full = h[:, fc % 2]
                        nc.vector.tensor_tensor(full, sil[:, fc % 2], sums[:, 1, fc % 2], ALU.mult).then_inc(hid_order, 1)
                        dve.wait_ge(hid_order, e * (2 * STEPS) + (2 * step + 1))
                        nc.vector.tensor_copy(h_parts[:, fc, 0:CT], full).then_inc(hid_order, 1)
                        dve.wait_ge(hid_order, e * (2 * STEPS) + (2 * step + 2))
                        for at, (_, c0, c1) in zip((CT + CAP[0], CT), SPLIT):
                            ins = nc.vector.tensor_tensor(h_parts[:, fc, at:at + c1 - c0], full[:, c0:c1],
                                                          h_parts[:, fc, c0:c1].bitcast(F32), ALU.subtract)
                        ins.then_inc(hid_done, 1)
                    if n + LEAD < FS * NU:
                        split(e, (n + LEAD) // NU, (n + LEAD) % NU)
                    elif after:
                        split(e + 1, 0, (n + LEAD) % NU)
                    if before and n in (0, 2):
                        weigh(e - 1, n // 2)
                    if after and n == FS * NU - 5:
                        split_x(e + 1)

            for b, (r, _, _) in enumerate(SPLIT):
                for half in range(2):
                    dve.wait_ge(gain_mm, 2 * b + half + 1)
                    nc.vector.tensor_copy(gain[:, r, 512 * half:512 * half + 512],
                                          y_banks[b][:, 512 * half:512 * half + 512]).then_inc(gain_done, 1)
            for s in range(TURNS):
                drain_x(0, s)
            split_x(0)
            for n in range(LEAD):
                split(0, 0, n)
            body(0, False, True)
            body(1, True, True)
            with dve.Fori(2, NE - 1) as e:
                body(e, True, True)
            body(NE - 1, True, False)
            for b in range(2):
                weigh(NE - 1, b)

        @block.tensor
        def _(pe):
            def turn_x(e, s):
                if s >= 2 or not is_first(e):
                    pe.wait_ge(xT_act, e * TURNS + (s - 1 if s >= 2 else 0))
                    pe.wait_ge(xT_dve, e * TURNS + (s - 1 if s >= 2 else 0))
                if s in (0, 4):
                    wait_apart(pe, xe_in[s // 4], e * 16 + 16, sem("experts_pe_turns"))
                else:
                    pe.sem_inc(sem("experts_pe_turns"), 1)
                for kind in range(2):
                    b, parts = turned(s, kind)
                    for k, r, at, c0, c1 in parts:
                        mm = nc.tensor.transpose(spare(s, kind)[:, at:at + c1 - c0], xe[b][:, k * P:(k + 1) * P],
                                                 core.ident[0:CAP[r], 0:CAP[r]])
                mm.then_inc(x_turned, 1)

            def unit(e, n, before, after):
                fs, u = divmod(n, NU)
                kind, fc = UNITS[u]
                step = 4 * fs + fc
                pe.wait_ge(unit_lo, e * (FS * NU) + (n + 1))
                if kind == 0 and not (is_first(e) and step < 2):
                    pe.wait_ge(hid_done, e * STEPS + (step - 1))
                if kind == 0 and after and 0 <= step - TURN0 < TURNS:
                    turn_x(e + 1, step - TURN0)
                if kind == 2:
                    pe.wait_ge(hid_done, e * STEPS + (step + 1))
                    if before and step == 0:
                        pe.wait_ge(y_done[0], e)
                        pe.wait_ge(y_done[1], e)
                if kind < 2:
                    out = core.ps[2 * (fc % 2) + kind]
                    for k in range(KD):
                        block = slice(k * P, (k + 1) * P)
                        nc.tensor.matmul(out[:, 0:2 * CT], w_hi[:, u, block], x[:, k, :], start=k == 0, stop=False)
                        mm = nc.tensor.matmul(out[:, 0:CT], w_lo[:, u, block], x[:, k, 0:CT], start=False, stop=k == KD - 1)
                else:
                    for b, tokens, w, first in ((0, sample_hi, w_hi, True), (0, sample_lo, w_hi, False),
                                                (0, sample_hi, w_lo, False), (1, prompt_pair, w_hi, True),
                                                (1, prompt_hi, w_lo, False)):
                        rows, last = tokens.stop - tokens.start, w is w_lo
                        for half in range(2):
                            cols = slice(512 * half, 512 * half + 512)
                            mm = nc.tensor.matmul(y_banks[b][0:rows, cols], h_parts[:, fc, tokens], w[:, u, cols],
                                                  start=step == 0 and first, stop=step == STEPS - 1 and last,
                                                  skip_group_check=True)
                mm.then_inc(unit_used, 1)

            def body(e, before, after):
                pe.wait_ge(x_split, e * 2 + 2)
                for n in range(FS * NU):
                    unit(e, n, before, after)

            for b, (r, _, _) in enumerate(SPLIT):
                for half in range(2):
                    for k in range(4 * half, 4 * half + 4):
                        mm = row_of(nc, y_banks[b][:, 512 * half:512 * half + 512], core.mod[:, 5 * KD + k, r:r + 1], k, r,
                                    core.ident)
                    mm.then_inc(gain_mm, 1)
            for s in range(TURNS):
                turn_x(0, s)
            pe.wait_ge(gain_done, 4)
            body(0, False, True)
            with pe.Fori(1, NE - 1) as e:
                body(e, True, True)
            body(NE - 1, True, False)


def final(core, A):
    nc, io, sem = core.nc, core.io, core.sem
    x = [A.at(D * j, D) for j in range(4)]
    y = [A.at(D * (4 + j), D) for j in range(4)]
    weight, junk = A.at(8 * D, D), A.at(9 * D, D)
    ss, rms, rstd = (core.small(f"final_{n}", [P, 4]) for n in ("ss", "rms", "rstd"))
    x_in, stored = ([sem(f"{n}{j}") for j in range(4)] for n in ("final_in", "final_out"))
    row_mm, row_done, act_order, root, y_done, x_free = (
        sem(n) for n in ("final_row_mm", "final_row", "final_act_order", "final_root", "final_y", "final_free"))

    def tiles(eng, body):
        for r, (lo, hi) in enumerate(TILES):
            if hi - lo == 4:
                for j in range(4):
                    body(lo + j, j, r)
            else:
                with eng.Fori(lo // 4, hi // 4) as turn:
                    for j in range(4):
                        body(turn * 4 + j, j, r)

    with nc.Block() as block:
        @block.sync
        def _(sp):
            def body(g, j, r):
                sp.wait_ge(x_free, g + 1)
                sp.dma_start(x[j], core.residual[bass.ds(g * P, P), :]).then_inc(x_in[j], 16)
            tiles(sp, body)

        @block.gpsimd
        def _(pool):
            def body(g, j, r):
                pool.wait_ge(y_done, g + 1)
                out = (io["y_prompt"], io["y_sample"])[r][0]
                pool.dma_start(out[bass.ds((g - TILES[r][0]) * P, P), :], y[j]).then_inc(stored[j], 16)
            tiles(pool, body)
            for j in range(4):
                pool.wait_ge(stored[j], NT // 4 * 16)

        @block.scalar
        def _(act):
            def body(g, j, r):
                act.wait_ge(x_in[j], (g - j) * 4 + 16)
                nc.scalar.activation(junk, x[j], ACT.Square, accum_out=ss[:, j:j + 1]).then_inc(act_order, 1)
                act.wait_ge(act_order, g + 1)
                nc.scalar.activation(rms[:, j:j + 1], ss[:, j:j + 1], ACT.Sqrt, bias=core.eps[:, 0:1],
                                     scale=1.0 / D).then_inc(root, 1)
            tiles(act, body)

        @block.vector
        def _(dve):
            dve.sem_inc(x_free, 4)
            for half in range(2):
                dve.wait_ge(row_mm, half + 1)
                nc.vector.tensor_copy(weight[:, 512 * half:512 * half + 512], core.ps[half]).then_inc(row_done, 1)
            dve.wait_ge(row_done, 2)

            def body(g, j, r):
                dve.wait_ge(root, g + 1)
                nc.vector.reciprocal(rstd[:, j:j + 1], rms[:, j:j + 1]).then_inc(sem("final_rstd"), 1)
                if not (isinstance(g, int) and g < 4):
                    dve.wait_ge(stored[j], (g - j) * 4)
                dve.wait_ge(sem("final_rstd"), g + 1)
                nc.vector.scalar_tensor_tensor(out=y[j], in0=x[j], scalar=rstd[:, j:j + 1], in1=weight, op0=ALU.mult,
                                               op1=ALU.mult).then_inc(y_done, 1)
                dve.wait_ge(y_done, g + 1)
                dve.sem_inc(x_free, 1)
            tiles(dve, body)

        @block.tensor
        def _(pe):
            for half in range(2):
                for k in range(4 * half, 4 * half + 4):
                    mm = row_of(nc, core.ps[half], core.col("final", k), k, 0, core.ident)
                mm.then_inc(row_mm, 1)


STAGES = [modulation, projections, convolution, states, ssd, attend, output, choice, experts, final]


def encoder_layer(nc, io, stages=None):
    with ExitStack() as ctx:
        core = Core(nc, ctx, io)
        stages = list(stages or STAGES)
        while stages:
            with ExitStack() as memory:
                arena = None
                if stages[0] is not experts:
                    arena = Arena(memory.enter_context(nc.sbuf_tensor("arena_" + stages[0].__name__, [P, ARENA], F32)), ARENA)
                while stages:
                    stage = stages.pop(0)
                    if stage is output:
                        core.release()
                    with ExitStack() as core.stage:
                        stage(core, arena)
                    if stage is experts or (stages and stages[0] is experts):
                        break
        core.release()


_BIG = ["x_prompt", "x_sample", "w_ada", "w_in", "w_uq", "w_ukv", "w_out", "w_router", "w_gate", "w_up", "w_down"]
_OUTS = [("y_prompt", (1, 512, 1024)), ("y_sample", (1, 1024, 1024))]


def packed(inputs):
    import numpy as np

    names = [("c_prompt",), ("c_sample",), ("norm1_w",), ("norm2_w",), ("final_norm_w",), ("q_norm_w",),
             ("kv_norm_w",), ("attn_norm_w",), ("ssd_norm_w",), ("conv_b",), ("conv_w",), ("b_ada",)]
    rows = np.concatenate([np.asarray(inputs[n[0]]).reshape(-1, P) for n in names])
    k, m = np.arange(P)[:, None], np.arange(P)[None, :]
    masks = np.stack([k == m, k <= m, k > m, k >= m, k < m, k < P + m], axis=1).astype(np.float32)
    vec = np.concatenate([np.asarray(inputs[n]).reshape(-1) for n in ("dt_bias", "a_log", "d_skip")])
    inv = (1.0 / (10000.0 ** (np.arange(0, DR, 2, dtype=np.float32) / DR))).astype(np.float32)
    ang = np.arange(1024, dtype=np.float32)[:, None] * inv[None, :]
    rope = np.stack([np.cos(ang), np.sin(ang)], axis=1).astype(np.float32)
    return {
        "p_cols": np.ascontiguousarray(rows.T),
        "p_masks": np.ascontiguousarray(masks),
        "p_rows": np.ascontiguousarray(np.broadcast_to(vec, (P, NROW))),
        "p_rope": np.ascontiguousarray(rope.reshape(8, P, 2, 16).transpose(1, 0, 2, 3)),
    }


def kernel(**inputs):
    import numpy as np
    import concourse.bacc as bacc
    from concourse.bass_utils import run_bass_kernel_spmd

    nc = bacc.Bacc("TRN2", target_bir_lowering=False, num_devices=1)
    arrays = {n: np.ascontiguousarray(inputs[n]) for n in _BIG}
    arrays.update(packed(inputs))
    io = {n: nc.dram_tensor(n, a.shape, mybir.dt.from_np(a.dtype), kind="ExternalInput").ap() for n, a in arrays.items()}
    for name, shape in _OUTS:
        io[name] = nc.dram_tensor(name, shape, F32, kind="ExternalOutput").ap()
    encoder_layer(nc, io)
    r = run_bass_kernel_spmd(nc, [arrays], core_ids=[0])
    return tuple(r.results[0][name] for name, _ in _OUTS)
```
